# Optimizing a Trainium2 kernel written in Bass

```python
import math
import jax
import jax.numpy as jnp
from jax import lax
import numpy as np

D_MODEL = 1024
BATCH = 1
SEQ = 128
DEPTH = 2
DEC_BATCH = 1
DEC_SEQ = 256
PAST_LEN = 128

GRID_W = 64
N_MIXERS = 2
N_HYENA_LAYERS = (DEPTH + 1) // 2
N_ATTN_LAYERS = DEPTH // 2
SHORT_CONV = 3
FILTER_HIDDEN = 64
N_BANDS = 16
POS_EMB_DIM = 1 + 2 * N_BANDS
DECAY_TARGET = 1e-2
FAST_DECAY_PCT = 0.3
SLOW_DECAY_PCT = 1.5
N_HEADS = 16
HEAD_DIM = D_MODEL // N_HEADS
WIN_ROWS = 8
WIN_COLS = 16
Q_BLOCK = 128
N_GROUPS = 4
EXPERTS_PER_GROUP = 4
N_EXPERTS = N_GROUPS * EXPERTS_PER_GROUP
TOP_K = 2
D_EXPERT = 512
DEEPNORM_ALPHA = (2 * DEPTH) ** 0.25
DEEPNORM_BETA = (8 * DEPTH) ** -0.25
LN_EPS = 1e-5

kernel_name = 'hybrid_hyena_natten_hmoe_diffusion_step'

def _layer_norm(x, g, b):
    xf = x.astype(jnp.float32)
    mu = jnp.mean(xf, axis=-1, keepdims=True)
    var = jnp.mean(jnp.square(xf - mu), axis=-1, keepdims=True)
    y = (xf - mu) * lax.rsqrt(var + LN_EPS) * g.astype(jnp.float32) + b.astype(jnp.float32)
    return y.astype(x.dtype)

def _adaln(cond, w, b):
    mod = jax.nn.silu(cond) @ w + b
    return [m[:, None, :] for m in jnp.split(mod, 6, axis=-1)]

def _modulate(x, shift, scale):
    return x * (1 + scale) + shift

def _short_conv(x, w, b):
    L = x.shape[1]
    pad = SHORT_CONV // 2
    xp = jnp.pad(x, ((0, 0), (pad, SHORT_CONV - 1 - pad), (0, 0)))
    y = b
    for j in range(SHORT_CONV):
        y = y + xp[:, j:j + L] * w[j]
    return y

def _hyena_filter(L, f_w1, f_b1, f_w2, f_b2, f_w3, f_freq, decay):
    pos = jnp.arange(L, dtype=jnp.float32)[:, None]
    t = pos / max(L - 1, 1)
    bands = jnp.linspace(1e-4, N_BANDS - 1, N_BANDS, dtype=jnp.float32)
    ang = (2.0 * math.pi / L) * pos * bands
    feat = jnp.concatenate([t, jnp.cos(ang), -jnp.sin(ang)], axis=-1)
    h = jnp.sin(f_freq * (feat @ f_w1 + f_b1))
    h = jnp.sin(f_freq * (h @ f_w2 + f_b2))
    h = (h @ f_w3).astype(jnp.float32) * jnp.exp(-t * jnp.abs(decay).astype(jnp.float32))
    return h[:, :D_MODEL], h[:, D_MODEL:]

def _bidir_long_conv(u, h_fwd, h_bwd):
    L = u.shape[1]
    n = 2 * L
    k = jnp.concatenate([h_fwd, jnp.zeros((1, D_MODEL), jnp.float32), h_bwd[1:][::-1]], axis=0)
    k_f = jnp.fft.rfft(k, n=n, axis=0)
    u_f = jnp.fft.rfft(u.astype(jnp.float32), n=n, axis=1)
    return jnp.fft.irfft(u_f * k_f[None], n=n, axis=1)[:, :L]

def _hyena(x, w_in, b_in, conv_w, conv_b, f_w1, f_b1, f_w2, f_b2, f_w3, f_freq, decay, d_skip, w_out, b_out):
    L = x.shape[1]
    z = _short_conv(x @ w_in + b_in, conv_w, conv_b)
    x0, x1, v = jnp.split(z, 3, axis=-1)
    h_fwd, h_bwd = _hyena_filter(L, f_w1, f_b1, f_w2, f_b2, f_w3, f_freq, decay)
    u = (v * x1).astype(jnp.float32)
    y = (_bidir_long_conv(u, h_fwd, h_bwd) + u * d_skip.astype(jnp.float32)) * x0.astype(jnp.float32)
    return y.astype(x.dtype) @ w_out + b_out

def _qkv(x, w, b):
    B, L, _ = x.shape
    q, k, v = jnp.split(x @ w + b, 3, axis=-1)
    split = lambda t: t.reshape(B, L, N_HEADS, HEAD_DIM).transpose(0, 2, 1, 3)
    return split(q), split(k), split(v)

def _merge_heads(t):
    B, H, L, Dh = t.shape
    return t.transpose(0, 2, 1, 3).reshape(B, L, H * Dh)

def _context_attention(q, k, v):
    B, H, L, Dh = q.shape
    nb = L // Q_BLOCK
    scale = HEAD_DIM ** -0.5
    qb = q.reshape(B, H, nb, Q_BLOCK, Dh).transpose(2, 0, 1, 3, 4)

    def block(qi):
        s = jnp.einsum('bhqd,bhkd->bhqk', qi, k).astype(jnp.float32) * scale
        p = jax.nn.softmax(s, axis=-1).astype(v.dtype)
        return jnp.einsum('bhqk,bhkd->bhqd', p, v)

    o = lax.map(block, qb)
    return o.transpose(1, 2, 0, 3, 4).reshape(B, H, L, Dh)

def _neighbourhood_attention(q, k, v, k_ctx, v_ctx, rpb):
    B, H, L, Dh = q.shape
    rows = L // GRID_W
    kh = min(WIN_ROWS, rows)
    kw = WIN_COLS
    scale = HEAD_DIM ** -0.5
    r = jnp.arange(rows)
    row_start = jnp.clip(r - kh // 2, 0, rows - kh)
    row_idx = row_start[:, None] + jnp.arange(kh)[None, :]
    col = jnp.arange(GRID_W)
    col_start = jnp.clip(col - kw // 2, 0, GRID_W - kw)
    in_band = (col[None, :] >= col_start[:, None]) & (col[None, :] < col_start[:, None] + kw)
    dr_idx = row_idx - r[:, None] + (WIN_ROWS - 1)
    dc_idx = jnp.clip(col[None, :] - col[:, None], -(kw - 1), kw - 1) + (WIN_COLS - 1)
    bias = rpb[:, dr_idx[:, None, :, None], dc_idx[None, :, None, :]].astype(jnp.float32)
    bias = jnp.where(in_band[None, None, :, None, :], bias, -jnp.inf)

    def one_request(args):
        qi, ki, vi, kci, vci = args
        qg = qi.reshape(H, rows, GRID_W, Dh)
        kr = ki.reshape(H, rows, GRID_W, Dh)[:, row_idx]
        vr = vi.reshape(H, rows, GRID_W, Dh)[:, row_idx]
        s_loc = jnp.einsum('hrqd,hrkwd->hrqkw', qg, kr).astype(jnp.float32) * scale + bias
        s_ctx = jnp.einsum('hrqd,hcd->hrqc', qg, kci).astype(jnp.float32) * scale
        m = jnp.maximum(jnp.max(s_loc, axis=(-2, -1)), jnp.max(s_ctx, axis=-1))
        e_loc = jnp.exp(s_loc - m[..., None, None])
        e_ctx = jnp.exp(s_ctx - m[..., None])
        denom = jnp.sum(e_loc, axis=(-2, -1)) + jnp.sum(e_ctx, axis=-1)
        p_loc = (e_loc / denom[..., None, None]).astype(vi.dtype)
        p_ctx = (e_ctx / denom[..., None]).astype(vi.dtype)
        o = jnp.einsum('hrqkw,hrkwd->hrqd', p_loc, vr) + jnp.einsum('hrqc,hcd->hrqd', p_ctx, vci)
        return o.reshape(H, L, Dh)

    return lax.map(one_request, (q, k, v, k_ctx, v_ctx))

def _hier_moe(x, w_group, b_group, w_expert, b_expert, w_up, w_down):
    B, L, D = x.shape
    t = x.reshape(B * L, D)
    g_logits = (t @ w_group + b_group).astype(jnp.float32)
    g_prob = jax.nn.softmax(g_logits, axis=-1)
    g_sel = jnp.argmax(g_logits, axis=-1)
    g_w = jnp.take_along_axis(g_prob, g_sel[:, None], axis=-1)
    e_logits = (t @ w_expert + b_expert).astype(jnp.float32).reshape(-1, N_GROUPS, EXPERTS_PER_GROUP)
    e_logits = jnp.take_along_axis(e_logits, g_sel[:, None, None], axis=1)[:, 0]
    e_prob = jax.nn.softmax(e_logits, axis=-1)
    top_w, top_i = lax.top_k(e_prob, TOP_K)
    top_w = top_w / jnp.sum(top_w, axis=-1, keepdims=True)
    expert_id = g_sel[:, None] * EXPERTS_PER_GROUP + top_i
    combine = jnp.sum(jax.nn.one_hot(expert_id, N_EXPERTS, dtype=jnp.float32) * (g_w * top_w)[..., None], axis=1)
    combine = combine.astype(x.dtype)
    y = jnp.zeros_like(t)
    for e in range(N_EXPERTS):
        a, b = jnp.split(t @ w_up[e], 2, axis=-1)
        y = y + combine[:, e:e + 1] * ((jax.nn.silu(a) * b) @ w_down[e])
    return y.reshape(B, L, D)

def _normal(key, shape, scale):
    return jax.random.normal(key, shape, jnp.float32) * scale

def setup_inputs(seed: int = 0) -> dict:
    key = jax.random.key(seed)
    ks = jax.random.split(key, 40)
    D = D_MODEL
    nh, na = N_HYENA_LAYERS, N_ATTN_LAYERS
    min_decay = math.log(DECAY_TARGET) / SLOW_DECAY_PCT
    max_decay = math.log(DECAY_TARGET) / FAST_DECAY_PCT
    decay0 = jnp.tile(jnp.linspace(min_decay, max_decay, D, dtype=jnp.float32), 2)
    return {
        'x_prompt': _normal(ks[0], (BATCH, SEQ, D), 1.0),
        'x_sample': _normal(ks[1], (DEC_BATCH, DEC_SEQ, D), 1.0),
        'cache_k': _normal(ks[2], (DEC_BATCH, na, N_HEADS, PAST_LEN, HEAD_DIM), 1.0),
        'cache_v': _normal(ks[3], (DEC_BATCH, na, N_HEADS, PAST_LEN, HEAD_DIM), 1.0),
        'c': _normal(ks[4], (DEC_BATCH, D), 1.0),
        'c_ctx': _normal(ks[5], (D,), 1.0),
        'w_ada': _normal(ks[6], (DEPTH, D, 6 * D), 0.5 * D ** -0.5),
        'b_ada': _normal(ks[7], (DEPTH, 6 * D), 0.02),
        'ln_g': 1.0 + _normal(ks[8], (DEPTH, 2, D), 0.02),
        'ln_b': _normal(ks[9], (DEPTH, 2, D), 0.02),
        'hy_w_in': _normal(ks[10], (nh, D, 3 * D), D ** -0.5),
        'hy_b_in': _normal(ks[11], (nh, 3 * D), 0.02),
        'hy_conv_w': _normal(ks[12], (nh, SHORT_CONV, 3 * D), SHORT_CONV ** -0.5),
        'hy_conv_b': _normal(ks[13], (nh, 3 * D), 0.02),
        'hy_f_w1': _normal(ks[14], (nh, POS_EMB_DIM, FILTER_HIDDEN), POS_EMB_DIM ** -0.5),
        'hy_f_b1': _normal(ks[15], (nh, FILTER_HIDDEN), 0.02),
        'hy_f_w2': _normal(ks[16], (nh, FILTER_HIDDEN, FILTER_HIDDEN), FILTER_HIDDEN ** -0.5),
        'hy_f_b2': _normal(ks[17], (nh, FILTER_HIDDEN), 0.02),
        'hy_f_w3': _normal(ks[18], (nh, FILTER_HIDDEN, 2 * D), 0.1 * FILTER_HIDDEN ** -0.5),
        'hy_f_freq': 1.0 + _normal(ks[19], (nh, FILTER_HIDDEN), 0.02),
        'hy_decay': decay0[None] + _normal(ks[20], (nh, 2 * D), 0.1),
        'hy_d': _normal(ks[21], (nh, D), 0.1),
        'hy_w_out': _normal(ks[22], (nh, D, D), DEEPNORM_BETA * D ** -0.5),
        'hy_b_out': _normal(ks[23], (nh, D), 0.02),
        'na_w_qkv': _normal(ks[24], (na, D, 3 * D), D ** -0.5),
        'na_b_qkv': _normal(ks[25], (na, 3 * D), 0.02),
        'na_rpb': _normal(ks[26], (na, N_HEADS, 2 * WIN_ROWS - 1, 2 * WIN_COLS - 1), 0.02),
        'na_w_out': _normal(ks[27], (na, D, D), DEEPNORM_BETA * D ** -0.5),
        'na_b_out': _normal(ks[28], (na, D), 0.02),
        'moe_w_group': _normal(ks[29], (DEPTH, D, N_GROUPS), D ** -0.5),
        'moe_b_group': _normal(ks[30], (DEPTH, N_GROUPS), 0.01),
        'moe_w_expert': _normal(ks[31], (DEPTH, D, N_EXPERTS), D ** -0.5),
        'moe_b_expert': _normal(ks[32], (DEPTH, N_EXPERTS), 0.01),
        'moe_w_up': _normal(ks[33], (DEPTH, N_EXPERTS, D, 2 * D_EXPERT), D ** -0.5),
        'moe_w_down': _normal(ks[34], (DEPTH, N_EXPERTS, D_EXPERT, D), DEEPNORM_BETA * D_EXPERT ** -0.5),
    }

def reference(x_prompt, x_sample, cache_k, cache_v, c, c_ctx, w_ada, b_ada, ln_g, ln_b,
              hy_w_in, hy_b_in, hy_conv_w, hy_conv_b, hy_f_w1, hy_f_b1, hy_f_w2, hy_f_b2, hy_f_w3,
              hy_f_freq, hy_decay, hy_d, hy_w_out, hy_b_out,
              na_w_qkv, na_b_qkv, na_rpb, na_w_out, na_b_out,
              moe_w_group, moe_b_group, moe_w_expert, moe_b_expert, moe_w_up, moe_w_down):
    yp = x_prompt
    ys = x_sample
    cond_ctx = c_ctx[None, :]
    new_k_layers = []
    new_v_layers = []
    for i in range(DEPTH):
        j = i // N_MIXERS
        sm_p, cm_p, gm_p, sf_p, cf_p, gf_p = _adaln(cond_ctx, w_ada[i], b_ada[i])
        sm_s, cm_s, gm_s, sf_s, cf_s, gf_s = _adaln(c, w_ada[i], b_ada[i])
        hp = _modulate(yp, sm_p, cm_p)
        hs = _modulate(ys, sm_s, cm_s)
        if i % N_MIXERS == 0:
            hy = (hy_w_in[j], hy_b_in[j], hy_conv_w[j], hy_conv_b[j], hy_f_w1[j], hy_f_b1[j], hy_f_w2[j],
                  hy_f_b2[j], hy_f_w3[j], hy_f_freq[j], hy_decay[j], hy_d[j], hy_w_out[j], hy_b_out[j])
            op = _hyena(hp, *hy)
            os_ = _hyena(hs, *hy)
        else:
            qp, kp, vp = _qkv(hp, na_w_qkv[j], na_b_qkv[j])
            op = _merge_heads(_context_attention(qp, kp, vp)) @ na_w_out[j] + na_b_out[j]
            new_k_layers.append(kp)
            new_v_layers.append(vp)
            qs, ks_, vs = _qkv(hs, na_w_qkv[j], na_b_qkv[j])
            att = _neighbourhood_attention(qs, ks_, vs, cache_k[:, j], cache_v[:, j], na_rpb[j])
            os_ = _merge_heads(att) @ na_w_out[j] + na_b_out[j]
        yp = _layer_norm(DEEPNORM_ALPHA * yp + gm_p * op, ln_g[i, 0], ln_b[i, 0])
        ys = _layer_norm(DEEPNORM_ALPHA * ys + gm_s * os_, ln_g[i, 0], ln_b[i, 0])
        moe = (moe_w_group[i], moe_b_group[i], moe_w_expert[i], moe_b_expert[i], moe_w_up[i], moe_w_down[i])
        fp = _hier_moe(_modulate(yp, sf_p, cf_p), *moe)
        fs = _hier_moe(_modulate(ys, sf_s, cf_s), *moe)
        yp = _layer_norm(DEEPNORM_ALPHA * yp + gf_p * fp, ln_g[i, 1], ln_b[i, 1])
        ys = _layer_norm(DEEPNORM_ALPHA * ys + gf_s * fs, ln_g[i, 1], ln_b[i, 1])
    new_k = jnp.stack(new_k_layers, axis=1)
    new_v = jnp.stack(new_v_layers, axis=1)
    return (yp, ys, new_k, new_v)


_drawn_inputs = setup_inputs


def setup_inputs(seed=0):
    import zlib

    import numpy as np

    out = dict(_drawn_inputs(seed))
    spreads = {}
    factors = {'cache_k': 6.262,
     'cache_v': 5.239,
     'hy_b_in': 23.334,
     'hy_conv_b': 23.684,
     'hy_f_b1': 8.0,
     'hy_f_b2': 8.0,
     'hy_f_freq': 25.355,
     'hy_decay': 21.646,
     'hy_d': 4.04,
     'hy_b_out': 8.0,
     'na_b_qkv': 3.008,
     'na_rpb': 64.0,
     'na_b_out': 8.0,
     'moe_b_group': 64.0,
     'moe_b_expert': 62.745}
    for name, (base, spread) in spreads.items():
        noise = np.random.default_rng([zlib.crc32(name.encode()), seed]).standard_normal(out[name].shape)
        drawn = base * np.exp(spread * noise) if base else spread * noise
        out[name] = jnp.asarray(drawn.astype(out[name].dtype))
    for name, factor in factors.items():
        out[name] = (out[name] * factor).astype(out[name].dtype)
    return out
```

```python
import math
from contextlib import ExitStack

import numpy as np
import concourse.bass as bass
from concourse import mybir

D = 1024
KT = D // 128
PROMPT, SAMPLE = 128, 256
TOK = PROMPT + SAMPLE
TT = TOK // 128
COND = [0, 1, 1]
DEPTH = 2
HEADS, DH = 16, 64
PAST = 128
GRID_W, ROWS, WIN_ROWS, WIN_COLS = 64, SAMPLE // 64, 8, 16
RPB_C = 2 * WIN_COLS - 1
RPB_H = (2 * WIN_ROWS - 1) * RPB_C
RPB_WIN = 5 * RPB_C + GRID_W
EXPERTS, GROUPS, PER_GROUP = 16, 4, 4
FE = 512
SLOT_TOK = 128
MAX_NB = TOK // SLOT_TOK
MAX_BLOCKS = 2 * TOK // SLOT_TOK + EXPERTS
FH, FEAT = 64, 33
ALPHA = (2 * DEPTH) ** 0.25
LN_EPS = 1e-5
PAD = TOK + 3
SEQ_AT = [(0, PROMPT, 1), (PROMPT, TOK, PROMPT + 2)]
TILE_AT = [1, PROMPT + 2, PROMPT + 2 + 128]
NEG = -1.0e30

RING = 6
ADA_W, IN_W, OUT_W, QKV_W = 12, 6, 2, 6
MOE_W = 3 * EXPERTS
W_AT, W_N = {}, {}
_at = 0
for _name, _n in [("ada0", ADA_W), ("in", IN_W), ("out0", OUT_W), ("moe0", MOE_W),
                  ("ada1", ADA_W), ("qkv", QKV_W), ("out1", OUT_W), ("moe1", MOE_W)]:
    W_AT[_name], W_N[_name] = _at, _n
    _at += _n

G_AT = {}
_at = 0
for _name, _n in [("vec", 2), ("ada0", 24), ("mlp", 2), ("filt", 12), ("filtK", 12), ("gm0", 4), ("xm0", 8),
                  ("in", 24), ("ut", 6), ("dft", 12), ("inv", 8), ("out0", 6), ("gf0", 4), ("xf0", 8),
                  ("logit0", 1), ("rank0", 1), ("tok0", 6),
                  ("ada1", 24), ("gm1", 4), ("xm1", 8), ("qk", 16), ("v", 6), ("kout", 2), ("kctx", 2),
                  ("ot", 8), ("out1", 6), ("gf1", 4), ("xf1", 8), ("logit1", 1), ("rank1", 1), ("tok1", 6)]:
    G_AT[_name] = _at
    _at += _n



def ada_groups(s):
    return (0 if s == 0 else 2 * s - 1), min(2 * s + 2, 2 * ADA_W - 1)


V_ADA, V_CC, V_CS, V_BQK = 0, 96, 104, 112
V_BIN, V_CW, V_CB = 128, 152, 224
DFT_COLS = 2560
MC_TRI, MC_ONES, MC_BEFORE, MC_THR = 0, 128, 256, 512
MC_PREF = MC_THR + MAX_NB
MC_COLS = MC_PREF + 4


def shape_constants():
    def tables(L):
        w = 2 * np.pi * (np.arange(L) + 0.5) / (2 * L)
        a = np.outer(np.arange(L), w)
        return np.cos(a), np.sin(a)

    def tiles(m):
        return m.reshape(m.shape[0] // 128, 128, m.shape[1]).transpose(1, 0, 2).reshape(128, -1)

    cs, ss = tables(SAMPLE)
    cp, sp = tables(PROMPT)
    dft = np.concatenate([tiles(cs), tiles(ss), tiles(cs.T / SAMPLE), tiles(ss.T / SAMPLE),
                          cp, sp, cp.T / PROMPT, sp.T / PROMPT], axis=1).astype(np.float32)
    feats, ts = [], []
    for L in (PROMPT, SAMPLE):
        pos = np.arange(L, dtype=np.float32)[:, None]
        t = pos / np.float32(L - 1)
        bands = np.linspace(1e-4, 15, 16, dtype=np.float32)
        ang = np.float32(2.0 * math.pi / L) * pos * bands
        feats.append(np.concatenate([t, np.cos(ang), -np.sin(ang)], axis=-1))
        ts.append(t[:, 0])
    feat = np.concatenate(feats).T.astype(np.float32)
    cols = np.zeros((128, 8), np.float32)
    cols[:, 0:3] = -np.concatenate(ts).reshape(3, 128).T
    cols[:, 3:6] = 1.0
    cols[0, 3] = cols[0, 4] = 0.0
    col = np.arange(GRID_W)
    start = np.clip(col - WIN_COLS // 2, 0, GRID_W - WIN_COLS)
    band = (col[None] >= start[:, None]) & (col[None] < start[:, None] + WIN_COLS)
    band = np.tile(np.where(band, 0.0, NEG), (2, 1)).astype(np.float32)
    moe = np.zeros((128, MC_COLS), np.float32)
    moe[:, MC_TRI:MC_TRI + 128] = np.triu(np.ones((128, 128)), 1)
    moe[:, MC_ONES:MC_ONES + 128] = 1.0
    moe[:, MC_BEFORE:MC_BEFORE + 256] = np.tril(np.ones((16, 16)), -1).reshape(-1)
    moe[:, MC_THR:MC_THR + MAX_NB] = np.arange(MAX_NB) * SLOT_TOK
    moe[:, MC_PREF:MC_PREF + 4] = [4, 3, 2, 1]
    return {"k_ident": np.eye(128, dtype=np.float32), "k_dft": dft, "k_feat": feat, "k_cols": cols,
            "k_band": band, "k_moe": moe}


def build(nc, A, y_prompt, y_sample, new_k, new_v):
    f32, i32 = mybir.dt.float32, mybir.dt.int32
    ACT = mybir.ActivationFunctionType
    ALU = mybir.AluOpType
    AX = mybir.AxisListType.X

    ctx = ExitStack()
    with ctx:
        origin = (nc.sbuf_base + 31) // 32 * 32

        def at(name, shape, offset, dt=f32):
            return nc.alloc_sbuf_tensor_at(name, shape, dt, offset=origin + offset)

        RA = RING * 16384
        RX0 = RA + 12288 + 12384
        RTOK = RX0 + 12384
        RK = RTOK + 12288
        RM = RK + 24576
        RS = RM + 15872
        ring = [at(f"ring{r}", [128, 4096], r * 16384) for r in range(RING)]
        hT = at("hT", [128, KT, TOK], RA)
        uT = at("uT", [128, KT, PAD], RA + 12288)
        hsum = at("hsum", [128, 3, D], RA)
        hdif = at("hdif", [128, 3, D], RA + 12288)
        feat = at("feat", [FEAT, TOK], RA)
        marg = at("marg", [FH, TOK], RA + 1536)
        mrnd = at("mrnd", [FH, TOK], RA + 3072)
        mh1 = at("mh1", [FH, TOK], RA + 4608)
        fw1 = at("fw1", [FEAT, FH], RA + 6144)
        fw2 = at("fw2", [FH, FH], RA + 6400)
        Y = at("Y", [128, 3, 2, D], RA)
        otok = at("otok", [128, TT, D], RA)
        kT = at("kT", [128, KT, TOK], RA + 12288)
        gath = at("gath", [128, 2, TT, D], RA)
        x0T = at("x0T", [128, KT, PAD], RX0)
        dabs = at("dabs", [128, 2 * D], RX0)
        mh2 = at("mh2", [FH, TOK], RX0 + 8192)
        V1 = at("V1", [128, 128], RX0 + 9728)
        V2 = at("V2", [128, 128], RX0 + 10240)
        qT = at("qT", [128, KT, TOK], RX0)
        oT = at("oT", [128, KT, TOK], RX0)
        mc = at("mc", [128, MC_COLS], RX0)
        tok = at("tok", [128, TT, D], RTOK)
        fw3 = at("fw3", [FH, 2 * D], RTOK)
        ftmp = at("ftmp", [128, 2, 512], RTOK + 8192)
        zt = at("zt", [128, 2, PAD + 1], RTOK)
        acc = at("acc", [128, 2, PAD + 1], RTOK + 2 * (PAD + 1) * 4)
        yT = at("yT", [128, KT, TOK], RTOK)
        decay = at("decay", [128, 3, 2 * D], RK)
        K = at("K", [128, 3, 2, D], RK)
        rows = at("rows", [128, 3, D], RK)
        rpb = at("rpb", [128, HEADS, RPB_WIN], RK)
        bm = at("bm", [128, 4, 256], RK + 14336)
        kraw = at("kraw", [128, D], RK + 18432)
        dft = at("dft", [128, DFT_COLS], RM)
        tmp = at("tmp", [128, 2, 512], RM + 10240)
        vctx = at("vctx", [128, D], RM)
        kctxT = at("kctxT", [128, KT, 128], RM + 4096)
        P = at("P", [128, 3, 384], RM + 8192)
        PT = at("PT", [128, 2, 384], RM + 12800)
        bv = at("bv", [128, D], RM + 8192)
        kst = at("kst", [128, D], RK + 20480)
        wr = at("wr", [128, KT, 20], RM)
        br = at("br", [128, 20], RM + 640)
        Lg = at("Lg", [128, TT, 20], RM + 768)
        ohg = at("ohg", [128, TT, 4], RM + 1024)
        o1 = at("o1", [128, TT, 4], RM + 1088)
        o2 = at("o2", [128, TT, 4], RM + 1152)
        esel = at("esel", [128, TT, 4], RM + 1216)
        sc4 = at("sc4", [128, TT, 4], RM + 1280)
        mx = at("mx", [128, 8, TT], RM + 1344)
        ex = at("ex", [128, 15], RM + 1472)
        M1 = at("M1", [128, TT, 16], RM + 1536)
        M2 = at("M2", [128, TT, 16], RM + 1728)
        Msel = at("Msel", [128, TT, 16], RM + 1920)
        R = at("R", [128, 64], RM + 2112)
        t48 = at("t48", [128, TT, 16], RM + 2560)
        nbase = at("nbase", [128, 33], RM + 2752)
        t256 = at("t256", [128, 256], RM + 2912)
        NBi = at("NBi", [128, 33], RM + 3936, i32)
        idxf = at("idxf", [128, 2, TT], RM + 4096)
        idx = at("idx", [128, 2, TT], RM + 4128, i32)
        pos = at("pos", [128, TT, 16], RM + 4160)
        wk = at("wk", [128, 2, TT], RM + 4352)
        xg = at("xg", [128, KT, SLOT_TOK], RM + 5888)
        sa = at("sa", [128, 4, SLOT_TOK], RM + 9984)
        he = at("he", [128, 4, SLOT_TOK], RM + 12032)
        xraw = at("xraw", [SLOT_TOK, D], RK + 12288)
        ysb = at("ysb", [SLOT_TOK, D], RK + 16384)
        arow = [at(f"arow{l}", [2, 2, 512], (RA + 12288, RX0)[l]) for l in range(2)]
        o = RS
        x = at("x", [128, TT, D], o); o += 12288
        gate = at("gate", [128, 2, D], o); o += 8192
        ident = at("ident", [128, 128], o); o += 512
        VT = at("VT", [128, 248], o); o += 992
        mod = [at(f"mod{l}", [128, 48, 2], o + 384 * l) for l in range(2)]; o += 768
        scond = at("scond", [128, KT, 2], o); o += 64
        cols = at("cols", [128, 8], o); o += 32
        band = at("band", [128, GRID_W], o); o += 256
        fcol = at("fcol", [FH, 4], o); o += 32
        st = at("st", [128, TT, 2, 6], o); o += 160
        mv = at("mv", [128, TT, 2], o); o += 32
        sd = at("sd", [128, 2, TT], o); o += 32
        nmax = at("nmax", [128, 48], o); o += 192
        den = at("den", [128, 48], o); o += 192
        rden = at("rden", [128, 48], o); o += 192
        credit = at("credit", [128, 8], o); o += 32
        assert origin + o <= nc.sbuf_usable_end, (origin + o, nc.sbuf_usable_end)

        ps = [ctx.enter_context(nc.psum_tensor(f"bank{i}", [128, 512], f32)) for i in range(8)]
        slots = nc.dram_tensor("slots", [(MAX_BLOCKS + 2) * SLOT_TOK, D], f32).ap()

        def sem(name):
            return ctx.enter_context(nc.semaphore(name))

        w_loaded = [sem(f"w_loaded{r}") for r in range(RING)]
        expert_done = [sem(f"expert_done{l}") for l in range(DEPTH)]
        group_ready = sem("group_ready")
        evacuated = [sem(f"evacuated{b}") for b in range(8)]
        first_in, x_in, filt_in, rows_in, moe_in, att_in, dft_in = (
            sem(n) for n in ("first_in", "x_in", "filt_in", "rows_in", "moe_in", "att_in", "dft_in"))
        scond_ready, mod_ready, cond_cols = sem("scond_ready"), sem("mod_ready"), sem("cond_cols")
        marg_ready, mh_ready, decay_ready, taps_ready = (
            sem(n) for n in ("marg_ready", "mh_ready", "decay_ready", "taps_ready"))
        dabs_ready, guards_ready, z_ready, z_used, u_ready, Y_ready = (
            sem(n) for n in ("dabs_ready", "guards_ready", "z_ready", "z_used", "u_ready", "Y_ready"))
        var_ready, sd_ready, ln_done, dve_step = sem("var_ready"), sem("sd_ready"), sem("ln_done"), sem("dve_step")
        ex_ready, ex_done, M_ready, nb_ready, idx_ready = (
            sem(n) for n in ("ex_ready", "ex_done", "M_ready", "nb_ready", "idx_ready"))
        s_ready, max_ready, p_ready, t_ready, pt_ready, pv_done, o_evac, bm_ready = (
            sem(n) for n in ("s_ready", "max_ready", "p_ready", "t_ready", "pt_ready", "pv_done", "o_evac", "bm_ready"))
        kv_out = sem("kv_out")
        zero_ready, zeros_out = sem("zero_ready"), sem("zeros_out")
        all_stored = sem("all_stored")
        blocks_done = sem("blocks_done")
        y_out = sem("y_out")
        moe_sems = []
        for l in range(DEPTH):
            moe_sems.append({n: sem(f"{n}{l}") for n in (
                "slots_filled", "xraw_in", "flip_ready", "xg_ready", "a_ready", "sa_ready", "b_ready", "he_ready",
                "y0_ready", "y1_ready", "ysb0_ready", "ysb1_ready", "y_stored", "rows_back")})

        block = ctx.enter_context(nc.Block())

        def w_view(i, k, n):
            return ring[i % RING][:, :].rearrange("p (k n) -> p k n", k=k)

        def wait_weights(eng, i):
            eng.wait_ge(w_loaded[i % RING], 16 * (i // RING + 1))

        def wait_group(eng, g):
            eng.wait_ge(group_ready, g + 1)

        def wait_evacuated(eng, g):
            eng.wait_ge(evacuated[g % 8], g // 8 + 1)

        def wait_all_evacuated(eng, end):
            for g in range(end - 8, end):
                wait_evacuated(eng, g)

        @block.sync
        def _(sp):
            def last_group(j):
                for name, group, groups in (("ada0", "ada0", 1), ("in", "in", 4), ("out0", "out0", TT),
                                            ("ada1", "ada1", 1), ("qkv", "qk", 4), ("out1", "out1", TT)):
                    s = j - W_AT[name]
                    if 0 <= s < W_N[name]:
                        if name[:3] == "ada":
                            return G_AT[name] + ada_groups(s)[0]
                        if name == "qkv" and s >= 4:
                            return G_AT["v"] + TT * (s - 4) + TT - 1
                        return G_AT[group] + groups * s + groups - 1

            def wait_slot_free(i):
                j = i - RING
                if j < 0:
                    return
                for l in range(DEPTH):
                    m = W_AT[f"moe{l}"]
                    if m <= j < m + MOE_W:
                        sp.wait_ge(expert_done[l], (j - m) // 3 + 1)
                        return
                sp.wait_ge(group_ready, last_group(j) + 1)

            def load(i, src, k):
                wait_slot_free(i)
                sp.dma_start(w_view(i, k, 4096 // k), src.rearrange("(k p) n -> p k n", p=128)
                             ).then_inc(w_loaded[i % RING], 16)

            def experts(l):
                up, down = A["moe_w_up"][l], A["moe_w_down"][l]
                first = W_AT[f"moe{l}"]

                def piece(i, src, k, n, value):
                    sp.dma_start(w_view(i, k, n), src.rearrange("o (k p) n -> p (o k) n", p=128)
                                 ).then_inc(w_loaded[i % RING], 16)

                def expert(e, i0, free):
                    for c in range(3):
                        free(c)
                        src = (up[bass.ds(e, 1), :, c * FE:(c + 1) * FE] if c < 2 else down[bass.ds(e, 1), :, :])
                        piece(i0 + c, src, 8 if c < 2 else 4, 512 if c < 2 else 1024, None)

                for e in range(2):
                    expert(e, first + 3 * e, lambda c, e=e: wait_slot_free(first + 3 * e + c))
                with sp.Fori(1, EXPERTS // 2) as p:
                    for half in range(2):
                        expert(2 * p + half, first + 3 * half,
                               lambda c, half=half: sp.wait_ge(expert_done[l], 2 * p + half - 1) if c == 0 else None)

            sp.wait_ge(first_in, 128)
            for s in range(ADA_W):
                load(W_AT["ada0"] + s, A["w_ada"][0][:, s * 512:(s + 1) * 512], 8)
            for s in range(IN_W):
                load(W_AT["in"] + s, A["hy_w_in"][0][:, s * 512:(s + 1) * 512], 8)
            for s in range(OUT_W):
                load(W_AT["out0"] + s, A["hy_w_out"][0][:, s * 512:(s + 1) * 512], 8)
            experts(0)
            for s in range(ADA_W):
                load(W_AT["ada1"] + s, A["w_ada"][1][:, s * 512:(s + 1) * 512], 8)
            for s in range(QKV_W):
                load(W_AT["qkv"] + s, A["na_w_qkv"][0][:, s * 512:(s + 1) * 512], 8)
            for s in range(OUT_W):
                load(W_AT["out1"] + s, A["na_w_out"][0][:, s * 512:(s + 1) * 512], 8)
            experts(1)
            sp.wait_ge(ln_done, 4)
            sp.dma_start(y_prompt[0], x[:, 0, :]).then_inc(y_out, 16)
            sp.dma_start(y_sample[0].rearrange("(t p) d -> p t d", p=128), x[:, 1:3, :]).then_inc(y_out, 16)
            sp.wait_ge(y_out, 32)

        @block.gpsimd
        def _(pool):
            def row_to_all(dst, src, n):
                return pool.dma_start(dst, bass.AP(src.tensor, src.offset, [[0, 128], [1, n]]))

            pool.dma_start(feat[:], A["k_feat"]).then_inc(filt_in, 16)
            pool.dma_start(fw1[:], A["hy_f_w1"][0]).then_inc(filt_in, 16)
            pool.dma_start(fw2[:], A["hy_f_w2"][0]).then_inc(filt_in, 16)
            pool.dma_start(fw3[:], A["hy_f_w3"][0]).then_inc(filt_in, 16)
            pool.dma_start(cols[:], A["k_cols"]).then_inc(filt_in, 16)
            for i, n in enumerate(("hy_f_b1", "hy_f_b2", "hy_f_freq")):
                pool.dma_start(fcol[:, i:i + 1], A[n].rearrange("a (p o) -> p (a o)", o=1)).then_inc(filt_in, 16)
            row_to_all(dabs[:], A["hy_decay"], 2 * D).then_inc(filt_in, 16)
            pool.dma_start(dft[:], A["k_dft"]).then_inc(dft_in, 16)
            pool.dma_start(band[:], A["k_band"]).then_inc(dft_in, 16)
            pool.dma_start(tmp[0:1, :, :].rearrange("p a n -> p (a n)"), A["hy_d"]).then_inc(dft_in, 16)


            nc.gpsimd.memset(gate[:, 0, :], 0.0).then_inc(zero_ready, 1)
            pool.wait_ge(zero_ready, 1)
            pool.wait_ge(mod_ready, 1)
            pool.dma_start(slots.rearrange("(a p) d -> p a d", p=128),
                           gate[:, 0, :].unsqueeze(1).to_broadcast([128, (MAX_BLOCKS + 2) * SLOT_TOK // 128, D])
                           ).then_inc(zeros_out, 16)

            def load_rows(l, which, bias):
                if bias is not None:
                    row_to_all(rows[:, 0, :], bias, D).then_inc(rows_in, 16)
                row_to_all(rows[:, 1, :], A["ln_g"][l, which], D).then_inc(rows_in, 16)
                row_to_all(rows[:, 2, :], A["ln_b"][l, which], D).then_inc(rows_in, 16)

            def moe_side(l):
                S = moe_sems[l]
                pool.wait_ge(ln_done, 2 * l + 1)
                pool.dma_start(wr[:, :, 0:4], A["moe_w_group"][l].rearrange("(k p) n -> p k n", p=128)).then_inc(moe_in, 16)
                pool.dma_start(wr[:, :, 4:20], A["moe_w_expert"][l].rearrange("(k p) n -> p k n", p=128)).then_inc(moe_in, 16)
                row_to_all(br[:, 0:4], A["moe_b_group"][l], 4).then_inc(moe_in, 16)
                row_to_all(br[:, 4:20], A["moe_b_expert"][l], 16).then_inc(moe_in, 16)
                pool.dma_start(mc[:], A["k_moe"]).then_inc(moe_in, 16)
                load_rows(l, 1, None)
                pool.wait_ge(zeros_out, 16)
                wait_all_evacuated(pool, G_AT[f"tok{l}"] + 6)
                pool.wait_ge(idx_ready, l + 1)
                for k in range(2):
                    for t in range(TT):
                        nc.gpsimd.indirect_dma_start(
                            out=slots[:, :], out_offset=bass.IndirectOffsetOnAxis(ap=idx[:, k, t:t + 1], axis=0),
                            in_=tok[:, t, :], in_offset=None).then_inc(S["slots_filled"], 16)
                pool.wait_ge(all_stored, l + 1)
                for k in range(2):
                    for t in range(TT):
                        nc.gpsimd.indirect_dma_start(
                            out=gath[:, k, t, :], out_offset=None, in_=slots[:, :],
                            in_offset=bass.IndirectOffsetOnAxis(ap=idx[:, k, t:t + 1], axis=0)).then_inc(S["rows_back"], 16)

            pool.wait_ge(Y_ready, 6)
            load_rows(0, 0, A["hy_b_out"])
            moe_side(0)
            pool.wait_ge(ln_done, 2)
            for i in range(2):
                src = A["na_rpb_rev"]
                first = RPB_H - (WIN_ROWS - 3) * RPB_C - WIN_COLS - (RPB_WIN - 1) + i * RPB_C
                pool.dma_start(rpb[i * GRID_W:(i + 1) * GRID_W, :, :],
                               bass.AP(src.tensor, first, [[1, GRID_W], [RPB_H, HEADS], [1, RPB_WIN]])).then_inc(att_in, 16)
            pool.dma_start(kraw[:].rearrange("t (h d) -> t h d", d=DH),
                           A["cache_k"][0, 0].rearrange("h t d -> t h d")).then_inc(att_in, 16)
            pool.dma_start(vctx[:].rearrange("t (h d) -> t h d", d=DH),
                           A["cache_v"][0, 0].rearrange("h t d -> t h d")).then_inc(att_in, 16)
            row_to_all(bv[:], A["na_b_qkv"][:, 2 * D:3 * D], D).then_inc(att_in, 16)
            pool.wait_ge(att_in, 80)
            pool.wait_ge(dft_in, 48)
            for n in range(2 * HEADS):
                if n >= 4:
                    pool.wait_ge(max_ready, HEADS + n - 3)
                e0 = (2 - 2 * (n // HEADS)) * RPB_C
                win = rpb[:, n % HEADS, RPB_WIN - 1 - e0:RPB_WIN - e0]
                nc.gpsimd.tensor_tensor(
                    bm[:, n % 4, :].rearrange("p (r c) -> p r c", c=GRID_W),
                    bass.AP(win.tensor, win.offset, [list(win.ap[0]), [-RPB_C, ROWS], [-1, GRID_W]]),
                    band[:].unsqueeze(1).to_broadcast([128, ROWS, GRID_W]), ALU.add).then_inc(bm_ready, 1)
            pool.wait_ge(o_evac, 6)
            pool.wait_ge(kv_out, 32)
            load_rows(1, 0, A["na_b_out"])
            moe_side(1)

        @block.tensor
        def _(pe):
            def bank(g):
                if g >= 8:
                    wait_evacuated(pe, g - 8)
                return ps[g % 8]

            def mm(out, lhsT, rhs, first=True, last=True):
                return nc.tensor.matmul(out, lhsT, rhs, start=first, stop=last)

            def ada(l):
                for n in range(ADA_W + 1):
                    if n < ADA_W:
                        i = W_AT[f"ada{l}"] + n
                        out = bank(G_AT[f"ada{l}"] + ada_groups(n)[0])
                        wait_weights(pe, i)
                        w = w_view(i, 8, 512)
                        for k in range(KT):
                            last = mm(out[0:2, :], scond[:, k, :], w[:, k, :], k == 0, k == KT - 1)
                        last.then_inc(group_ready, 1)
                    if n >= 1:
                        row, col = ada_groups(n - 1)
                        out = bank(G_AT[f"ada{l}"] + col)
                        wait_evacuated(pe, G_AT[f"ada{l}"] + row)
                        for f in range(4):
                            last = nc.tensor.transpose(out[:, 2 * f:2 * f + 2], arow[l][:, (n - 1) % 2, f * 128:(f + 1) * 128],
                                                       ident[0:2, 0:2])
                        last.then_inc(group_ready, 1)

            def gates(name, l, first_col):
                for c in range(2):
                    for h in range(2):
                        g = G_AT[name] + 2 * c + h
                        out = bank(g)
                        for j in range(4):
                            col = mod[l][:, first_col + 4 * h + j, c:c + 1]
                            last = mm(out[:, j * 128:(j + 1) * 128], col.to_broadcast([128, 128]), ident[:])
                        last.then_inc(group_ready, 1)

            def transpose_tiles(name, src, count):
                for j in range(count):
                    out = bank(G_AT[name] + j)
                    for t in range(TT):
                        last = nc.tensor.transpose(out[:, t * 128:(t + 1) * 128], src[:, t, j * 128:(j + 1) * 128], ident[:])
                    last.then_inc(group_ready, 1)

            def to_tokens(name, src):
                for t in range(TT):
                    for h in range(2):
                        out = bank(G_AT[name] + 2 * t + h)
                        for j in range(4):
                            last = nc.tensor.transpose(out[:, j * 128:(j + 1) * 128], src(4 * h + j, t), ident[:])
                        last.then_inc(group_ready, 1)

            pe.wait_ge(first_in, 128)
            out = bank(0)
            nc.tensor.transpose(out[:, 0:128], V1[:], ident[:]).then_inc(group_ready, 1)
            out = bank(1)
            nc.tensor.transpose(out[:, 0:120], V2[0:120, :], ident[0:120, 0:120]).then_inc(group_ready, 1)
            pe.wait_ge(scond_ready, 1)
            ada(0)

            pe.wait_ge(filt_in, 144)
            mm(bank(G_AT["mlp"])[0:FH, 0:TOK], fw1[:], feat[:]).then_inc(group_ready, 1)
            pe.wait_ge(mh_ready, 1)
            mm(bank(G_AT["mlp"] + 1)[0:FH, 0:TOK], fw2[:], mh1[:]).then_inc(group_ready, 1)
            pe.wait_ge(mh_ready, 2)
            for t in range(TT):
                for h in range(2):
                    for d in range(2):
                        mm(bank(G_AT["filt"] + 4 * t + 2 * h + d)[:, :], mh2[:, t * 128:(t + 1) * 128],
                           fw3[:, d * D + h * 512:d * D + (h + 1) * 512]).then_inc(group_ready, 1)

            Cs = dft[:, 0:512].rearrange("p (k f) -> p k f", k=2)
            Ss = dft[:, 512:1024].rearrange("p (k f) -> p k f", k=2)
            Ci = dft[:, 1024:1536].rearrange("p (k f) -> p k f", k=2)
            Si = dft[:, 1536:2048].rearrange("p (k f) -> p k f", k=2)
            Cp, Sp, Cpi, Spi = (dft[:, 2048 + 128 * q:2176 + 128 * q] for q in range(4))

            def spectrum(name, cos_src, sin_src):
                for q in range(3):
                    for h in range(2):
                        for r in range(2):
                            out = bank(G_AT[name] + 4 * q + 2 * h + r)
                            src = (cos_src, sin_src)[r]
                            cs = slice(h * 512, (h + 1) * 512)
                            if q == 0:
                                last = mm(out[:, :], (Cp, Sp)[r], src[:, 0, cs])
                            else:
                                for k in range(2):
                                    last = mm(out[:, :], (Cs, Ss)[r][:, k, (q - 1) * 128:q * 128], src[:, 1 + k, cs],
                                              k == 0, k == 1)
                            last.then_inc(group_ready, 1)

            pe.wait_ge(dft_in, 48)
            pe.wait_ge(taps_ready, 1)
            spectrum("filtK", hsum, hdif)

            pe.wait_ge(mod_ready, 1)
            gates("gm0", 0, 16)
            pe.wait_ge(x_in, 32)
            transpose_tiles("xm0", x, KT)
            wait_all_evacuated(pe, G_AT["in"])
            for s in range(IN_W):
                i = W_AT["in"] + s
                wait_weights(pe, i)
                w = w_view(i, 8, 512)
                for f in range(4):
                    out = bank(G_AT["in"] + 4 * s + f)
                    for k in range(KT):
                        last = mm(out[:, 0:TOK], w[:, k, f * 128:(f + 1) * 128], hT[:, k, :], k == 0, k == KT - 1)
                    last.then_inc(group_ready, 1)
            pe.wait_ge(u_ready, 1)
            to_tokens("ut", lambda j, t: uT[:, j, TILE_AT[t]:TILE_AT[t] + 128])
            wait_all_evacuated(pe, G_AT["dft"])
            spectrum("dft", tok, tok)
            pe.wait_ge(Y_ready, 6)
            for j in range(KT):
                out = bank(G_AT["inv"] + j)
                js = slice(j * 128, (j + 1) * 128)
                mm(out[:, 0:128], Y[:, 0, 0, js], Cpi, True, False)
                mm(out[:, 0:128], Y[:, 0, 1, js], Spi, False, True)
                n = 0
                for q in range(2):
                    for r in range(2):
                        last = mm(out[:, 128:TOK], Y[:, 1 + q, r, js], (Ci, Si)[r][:, q, :], n == 0, n == 3)
                        n += 1
                last.then_inc(group_ready, 1)
            wait_all_evacuated(pe, G_AT["out0"])

            def project_out(l, src):
                for h in range(2):
                    i = W_AT[f"out{l}"] + h
                    wait_weights(pe, i)
                    w = w_view(i, 8, 512)
                    for t in range(TT):
                        out = bank(G_AT[f"out{l}"] + TT * h + t)
                        for k in range(KT):
                            last = mm(out[:, :], src[:, k, t * 128:(t + 1) * 128], w[:, k, :], k == 0, k == KT - 1)
                        last.then_inc(group_ready, 1)

            def moe(l):
                S = moe_sems[l]
                pe.wait_ge(ln_done, 2 * l + 1)
                gates(f"gf{l}", l, 40)
                transpose_tiles(f"xf{l}", x, KT)
                wait_all_evacuated(pe, G_AT[f"logit{l}"])
                pe.wait_ge(moe_in, 80 * (l + 1))
                out = bank(G_AT[f"logit{l}"])
                for t in range(TT):
                    for k in range(KT):
                        last = mm(out[:, 20 * t:20 * t + 20], hT[:, k, t * 128:(t + 1) * 128], wr[:, k, :], k == 0, k == KT - 1)
                last.then_inc(group_ready, 1)
                pe.wait_ge(M_ready, l + 1)
                out = bank(G_AT[f"rank{l}"])
                tri, ones = mc[:, MC_TRI:MC_TRI + 128], mc[:, MC_ONES:MC_ONES + 128]
                for t in range(TT):
                    for u in range(t):
                        mm(out[:, 16 * t:16 * t + 16], ones, Msel[:, u, :], u == 0, False)
                    mm(out[:, 16 * t:16 * t + 16], tri, Msel[:, t, :], t == 0, True)
                for u in range(TT):
                    last = mm(out[:, 48:64], ones, Msel[:, u, :], u == 0, u == TT - 1)
                last.then_inc(group_ready, 1)
                to_tokens(f"tok{l}", lambda j, t: hT[:, j, t * 128:(t + 1) * 128])
                wait_all_evacuated(pe, G_AT[f"tok{l}"] + 6)
                pe.wait_ge(nb_ready, l + 1)
                first = W_AT[f"moe{l}"]

                def flip_block():
                    for k in range(KT):
                        last = nc.tensor.transpose(ps[(0, 5)[k // 4]][:, (k % 4) * 128:(k % 4 + 1) * 128],
                                                   xraw[:, k * 128:(k + 1) * 128], ident[:])
                    last.then_inc(S["flip_ready"], 1)

                pe.wait_ge(S["xraw_in"], 16)
                flip_block()
                with pe.Fori(0, EXPERTS // 2) as p:
                    for half in range(2):
                        i0 = first + 3 * half
                        nb = pe.value_load(NBi[0:1, bass.ds(2 * p + half, 1)], min_val=1, max_val=MAX_NB)
                        base = pe.value_load(NBi[0:1, bass.ds(2 * p + half + 16, 1)], min_val=0, max_val=MAX_BLOCKS)
                        for c in range(3):
                            pe.wait_ge(w_loaded[(i0 + c) % RING], 16 * p + 16 * ((i0 + c) // RING + 1))
                            mm(ps[7][:, 0:2], ident[:], ident[:, 0:2])
                        wa, wb, wd = w_view(i0, 8, 512), w_view(i0 + 1, 8, 512), w_view(i0 + 2, 4, 1024)
                        with pe.Fori(0, nb) as b:
                            w1 = base + b + 1
                            pe.wait_ge(S["xg_ready"], w1 * 2)
                            for out, w, name in ((ps[1], wa, "a_ready"), (ps[2], wb, "b_ready")):
                                for f in range(4):
                                    for k in range(KT):
                                        last = mm(out[:, f * SLOT_TOK:(f + 1) * SLOT_TOK], w[:, k, f * 128:(f + 1) * 128],
                                                  xg[:, k, :], k == 0, k == KT - 1)
                                last.then_inc(S[name], 1)
                            pe.wait_ge(S["xraw_in"], w1 * 16 + 16)
                            flip_block()
                            pe.wait_ge(S["he_ready"], w1)
                            for h in range(2):
                                for k in range(4):
                                    last = mm(ps[3 + h][0:SLOT_TOK, :], he[:, k, :], wd[:, k, h * 512:(h + 1) * 512],
                                              k == 0, k == 3)
                                last.then_inc(S[f"y{h}_ready"], 1)
                        mm(ps[7][:, 0:2], ident[:], ident[:, 0:2]).then_inc(expert_done[l], 1)
                pe.wait_ge(blocks_done, 2 * l + 2)

            project_out(0, yT)
            moe(0)

            ada(1)
            pe.wait_ge(mod_ready, 2)
            pe.wait_ge(ln_done, 2)
            gates("gm1", 1, 16)
            transpose_tiles("xm1", x, KT)
            wait_all_evacuated(pe, G_AT["qk"])
            for s in range(4):
                i = W_AT["qkv"] + s
                wait_weights(pe, i)
                w = w_view(i, 8, 512)
                for f in range(4):
                    out = bank(G_AT["qk"] + 4 * s + f)
                    for k in range(KT):
                        last = mm(out[:, 0:TOK], w[:, k, f * 128:(f + 1) * 128], hT[:, k, :], k == 0, k == KT - 1)
                    last.then_inc(group_ready, 1)
            for h in range(2):
                i = W_AT["qkv"] + 4 + h
                wait_weights(pe, i)
                w = w_view(i, 8, 512)
                for t in range(TT):
                    out = bank(G_AT["v"] + TT * h + t)
                    for k in range(KT):
                        last = mm(out[:, :], hT[:, k, t * 128:(t + 1) * 128], w[:, k, :], k == 0, k == KT - 1)
                    last.then_inc(group_ready, 1)
            pe.wait_ge(att_in, 80)
            for h in range(2):
                out = bank(G_AT["kout"] + h)
                for j in range(4):
                    last = nc.tensor.transpose(out[:, j * 128:(j + 1) * 128], kraw[:, (4 * h + j) * 128:(4 * h + j + 1) * 128], ident[:])
                last.then_inc(group_ready, 1)
            for h in range(2):
                out = bank(G_AT["kctx"] + h)
                for j in range(4):
                    last = nc.tensor.transpose(out[:, j * 128:(j + 1) * 128], kT[:, 4 * h + j, 0:128], ident[:])
                last.then_inc(group_ready, 1)
            wait_all_evacuated(pe, G_AT["ot"])

            units = TT * HEADS

            def scores(u):
                t, h = divmod(u, HEADS)
                lo = DH * (h % 2)
                if u >= 3:
                    pe.wait_ge(p_ready, u - 2)
                q = qT[lo:lo + DH, h // 2, t * 128:(t + 1) * 128]
                if t == 0:
                    last = mm(ps[u % 3][:, 0:128], q, kT[lo:lo + DH, h // 2, 0:PROMPT])
                else:
                    mm(ps[u % 3][:, 0:256], q, kT[lo:lo + DH, h // 2, PROMPT:TOK])
                    last = mm(ps[u % 3][:, 256:384], q, kctxT[lo:lo + DH, h // 2, :])
                last.then_inc(s_ready, 1)

            def flip(u):
                pe.wait_ge(p_ready, u + 1)
                if u >= 2:
                    pe.wait_ge(pt_ready, u - 1)
                for c in range(1 if u < HEADS else 3):
                    last = nc.tensor.transpose(ps[3 + u % 2][:, c * 128:(c + 1) * 128], P[:, u % 3, c * 128:(c + 1) * 128], ident[:])
                last.then_inc(t_ready, 1)

            def weigh(u):
                t, h = divmod(u, HEADS)
                half = u // 8
                if u % 8 == 0 and half >= 3:
                    pe.wait_ge(o_evac, half - 2)
                pe.wait_ge(pt_ready, u + 1)
                out = ps[5 + half % 3][:, (h % 8) * DH:(h % 8 + 1) * DH]
                hs = slice(h * DH, (h + 1) * DH)
                if t == 0:
                    last = mm(out, PT[:, u % 2, 0:128], tok[:, 0, hs])
                else:
                    mm(out, PT[:, u % 2, 0:128], tok[:, 1, hs], True, False)
                    mm(out, PT[:, u % 2, 128:256], tok[:, 2, hs], False, False)
                    last = mm(out, PT[:, u % 2, 256:384], vctx[:, hs], False, True)
                last.then_inc(pv_done, 1)

            for n in range(units + 3):
                if n < units:
                    scores(n)
                if 0 <= n - 2 < units:
                    flip(n - 2)
                if 0 <= n - 3 < units:
                    weigh(n - 3)
            pe.wait_ge(o_evac, 6)
            transpose_tiles("ot", otok, KT)
            wait_all_evacuated(pe, G_AT["out1"])
            project_out(1, oT)
            moe(1)

        @block.scalar
        def _(act):
            act.dma_start(V1[0:96, :], A["b_ada"].rearrange("l (f p) -> (l f) p", p=128)).then_inc(first_in, 16)
            act.dma_start(V1[96:104, :], A["c_ctx"].rearrange("(f p) -> f p", p=128)).then_inc(first_in, 16)
            act.dma_start(V1[104:112, :], A["c"].rearrange("a (f p) -> (a f) p", p=128)).then_inc(first_in, 16)
            act.dma_start(V1[112:128, :], A["na_b_qkv"][:, 0:2 * D].rearrange("a (f p) -> (a f) p", p=128)).then_inc(first_in, 16)
            act.dma_start(ident[:], A["k_ident"]).then_inc(first_in, 16)
            act.dma_start(V2[0:24, :], A["hy_b_in"].rearrange("a (f p) -> (a f) p", p=128)).then_inc(first_in, 16)
            act.dma_start(V2[24:96, :], A["hy_conv_w"][0].rearrange("j (f p) -> (j f) p", p=128)).then_inc(first_in, 16)
            act.dma_start(V2[96:120, :], A["hy_conv_b"].rearrange("a (f p) -> (a f) p", p=128)).then_inc(first_in, 16)
            act.dma_start(x[:, 0, :], A["x_prompt"][0]).then_inc(x_in, 16)
            act.dma_start(x[:, 1:3, :], A["x_sample"][0].rearrange("(t p) d -> p t d", p=128)).then_inc(x_in, 16)

            act.wait_ge(cond_cols, 1)
            nc.scalar.activation(scond[:, :, :].rearrange("p k c -> p c k"),
                                 VT[:, V_CC:V_CC + 16].rearrange("p (c k) -> p c k", c=2), ACT.Silu).then_inc(scond_ready, 1)

            def ada(l, first, end):
                for n in range(first, end):
                    if n < ADA_W:
                        g = G_AT[f"ada{l}"] + ada_groups(n)[0]
                        wait_group(act, g)
                        nc.scalar.activation(arow[l][:, n % 2, :], ps[g % 8][0:2, :], ACT.Copy).then_inc(evacuated[g % 8], 1)
                    if n >= 1:
                        g = G_AT[f"ada{l}"] + ada_groups(n - 1)[1]
                        wait_group(act, g)
                        nc.scalar.activation(mod[l][:, 4 * n - 4:4 * n, :].rearrange("p f c -> p (f c)"), ps[g % 8][:, 0:8],
                                             ACT.Copy).then_inc(evacuated[g % 8], 1)

            ada(0, 0, ADA_W + 1)

            act.wait_ge(marg_ready, 1)
            nc.scalar.activation(mh1[:], marg[:], ACT.Sin).then_inc(mh_ready, 1)
            act.wait_ge(marg_ready, 2)
            nc.scalar.activation(mh2[:], marg[:], ACT.Sin).then_inc(mh_ready, 1)
            act.wait_ge(dabs_ready, 1)
            for t in range(TT):
                nc.scalar.activation(decay[:, t, :], dabs[:], ACT.Exp, scale=cols[:, t:t + 1]).then_inc(decay_ready, 1)
            act.wait_ge(taps_ready, 1)
            for n in range(12):
                g = G_AT["filtK"] + n
                q, h, r = n // 4, n // 2 % 2, n % 2
                wait_group(act, g)
                nc.scalar.activation(K[:, q, r, h * 512:(h + 1) * 512], ps[g % 8][:, :], ACT.Copy).then_inc(evacuated[g % 8], 1)

            def modulate_odd(name, l, shift, scale):
                for j in range(1, KT, 2):
                    g = G_AT[name] + j
                    wait_group(act, g)
                    for c, (a, b) in enumerate(((0, PROMPT), (PROMPT, TOK))):
                        last = nc.scalar.activation(hT[:, j, a:b], ps[g % 8][:, a:b], ACT.Identity,
                                                    bias=mod[l][:, shift + j, c:c + 1], scale=mod[l][:, scale + j, c:c + 1])
                    last.then_inc(evacuated[g % 8], 1)

            act.wait_ge(mod_ready, 1)
            modulate_odd("xm0", 0, 0, 8)

            act.wait_ge(guards_ready, 1)
            for n in range(24):
                g = G_AT["in"] + n
                wait_group(act, g)
                if n >= 2:
                    act.wait_ge(z_used, n - 1)
                for a, b, at_ in SEQ_AT:
                    last = nc.scalar.activation(zt[:, n % 2, at_:at_ + b - a], ps[g % 8][:, a:b], ACT.Identity,
                                                bias=VT[:, V_BIN + n:V_BIN + n + 1])
                last.then_inc(evacuated[g % 8], 1)
            act.wait_ge(z_used, 24)
            act.wait_ge(u_ready, 1)
            for n in range(6):
                g = G_AT["ut"] + n
                wait_group(act, g)
                nc.scalar.activation(tok[:, n // 2, (n % 2) * 512:(n % 2 + 1) * 512], ps[g % 8][:, :], ACT.Copy
                                     ).then_inc(evacuated[g % 8], 1)

            def root(n):
                act.wait_ge(var_ready, n + 1)
                nc.scalar.activation(sd[:, 0, :], sd[:, 1, :], ACT.Sqrt).then_inc(sd_ready, 1)

            def moe(l):
                S = moe_sems[l]
                root(2 * l)
                modulate_odd(f"xf{l}", l, 24, 32)
                act.wait_ge(ex_ready, l + 1)
                nc.scalar.activation(ex[:], ex[:], ACT.Exp).then_inc(ex_done, 1)
                for n in range(6):
                    g = G_AT[f"tok{l}"] + n
                    wait_group(act, g)
                    nc.scalar.activation(tok[:, n // 2, (n % 2) * 512:(n % 2 + 1) * 512], ps[g % 8][:, :], ACT.Copy
                                         ).then_inc(evacuated[g % 8], 1)
                act.wait_ge(S["slots_filled"], 96)
                act.dma_start(xraw[:], slots[0:SLOT_TOK, :]).then_inc(S["xraw_in"], 16)
                act.wait_ge(S["flip_ready"], 1)
                nc.scalar.activation(xg[:, 4:8, :].rearrange("p k s -> p (k s)"), ps[5][:, :], ACT.Copy).then_inc(S["xg_ready"], 1)
                act.dma_start(xraw[:], slots[SLOT_TOK:2 * SLOT_TOK, :]).then_inc(S["xraw_in"], 16)
                act.wait_ge(nb_ready, l + 1)
                total = act.value_load(NBi[0:1, 32:33], min_val=EXPERTS, max_val=MAX_BLOCKS)
                with act.Fori(0, total) as b:
                    act.wait_ge(S["a_ready"], b + 1)
                    nc.scalar.activation(sa[:].rearrange("p f s -> p (f s)"), ps[1][:, 0:4 * SLOT_TOK], ACT.Silu
                                         ).then_inc(S["sa_ready"], 1)
                    act.wait_ge(S["flip_ready"], b + 2)
                    nc.scalar.activation(xg[:, 4:8, :].rearrange("p k s -> p (k s)"), ps[5][:, :], ACT.Copy).then_inc(S["xg_ready"], 1)
                    act.dma_start(xraw[:], slots[bass.ds(b * SLOT_TOK + 2 * SLOT_TOK, SLOT_TOK), :]).then_inc(S["xraw_in"], 16)
                    act.wait_ge(S["y1_ready"], b + 1)
                    act.wait_ge(S["y_stored"], b * 16 + 16)
                    nc.scalar.activation(ysb[:, 512:1024], ps[4][0:SLOT_TOK, :], ACT.Copy).then_inc(S["ysb1_ready"], 1)
                    act.wait_ge(S["ysb0_ready"], b + 1)
                    act.wait_ge(S["ysb1_ready"], b + 1)
                    act.dma_start(slots[bass.ds(b * SLOT_TOK, SLOT_TOK), :], ysb[:]).then_inc(S["y_stored"], 16)
                nc.scalar.activation(credit[:, 3:4], ident[:, 0:1], ACT.Copy).then_inc(blocks_done, 1)
                act.wait_ge(S["y_stored"], total * 16 + 16)
                act.wait_ge(S["xraw_in"], total * 16 + 32)
                nc.scalar.activation(credit[:, 1:2], ident[:, 0:1], ACT.Copy).then_inc(all_stored, 1)
                if l == 0:
                    act.wait_ge(blocks_done, 2)
                    ada(1, 0, 4)
                root(2 * l + 1)
                if l == 0:
                    ada(1, 4, ADA_W + 1)

            moe(0)

            act.wait_ge(mod_ready, 2)
            modulate_odd("xm1", 1, 0, 8)
            for j in range(KT):
                g = G_AT["qk"] + KT + j
                wait_group(act, g)
                nc.scalar.activation(kT[:, j, :], ps[g % 8][:, 0:TOK], ACT.Identity,
                                     bias=VT[:, V_BQK + KT + j:V_BQK + KT + j + 1]).then_inc(evacuated[g % 8], 1)
            for g in (G_AT["v"], G_AT["v"] + TT):
                wait_evacuated(act, g)
            act.dma_start(new_v[0, 0].rearrange("h t d -> t h d"), tok[:, 0, :].rearrange("t (h d) -> t h d", d=DH)
                          ).then_inc(kv_out, 16)
            for h in range(2):
                g = G_AT["kout"] + h
                wait_group(act, g)
                nc.scalar.activation(kctxT[:, 4 * h:4 * h + 4, :].rearrange("p j t -> p (j t)"), ps[g % 8][:, :], ACT.Copy
                                     ).then_inc(evacuated[g % 8], 1)
            for h in range(2):
                g = G_AT["kctx"] + h
                wait_group(act, g)
                nc.scalar.activation(kst[:, h * 512:(h + 1) * 512], ps[g % 8][:, :], ACT.Copy).then_inc(evacuated[g % 8], 1)
            for h in range(2):
                wait_evacuated(act, G_AT["kctx"] + h)
            act.dma_start(new_k[0, 0].rearrange("h t d -> t h d"), kst[:].rearrange("t (h d) -> t h d", d=DH)
                          ).then_inc(kv_out, 16)

            units = TT * HEADS

            def exponentials(u):
                n = 128 if u < HEADS else 384
                act.wait_ge(max_ready, u + 1)
                if u >= 3:
                    act.wait_ge(t_ready, u - 2)
                nc.scalar.activation(P[:, u % 3, 0:n], ps[u % 3][:, 0:n], ACT.Exp, bias=nmax[:, u:u + 1],
                                     accum_out=den[:, u:u + 1]).then_inc(p_ready, 1)

            def flipped(u):
                n = 128 if u < HEADS else 384
                act.wait_ge(t_ready, u + 1)
                if u >= 2:
                    act.wait_ge(pv_done, u - 1)
                nc.scalar.activation(PT[:, u % 2, 0:n], ps[3 + u % 2][:, 0:n], ACT.Copy).then_inc(pt_ready, 1)

            for n in range(units + 2):
                if n < units:
                    exponentials(n)
                if n >= 2:
                    flipped(n - 2)
            moe(1)
            act.wait_ge(kv_out, 32)

        @block.vector
        def _(dve):
            v = nc.vector
            steps = [0]

            def link(ins):
                steps[0] += 1
                ins.then_inc(dve_step, 1)
                dve.wait_ge(dve_step, steps[0])

            for g, n in ((0, 128), (1, 120)):
                wait_group(dve, g)
                last = v.tensor_copy(VT[:, 128 * g:128 * g + n], ps[g][:, 0:n])
                last.then_inc(evacuated[g], 1)
                if g == 0:
                    wait_evacuated(dve, 0)
                    v.memset(credit[:, 4:5], 0.0).then_inc(cond_cols, 1)
            wait_evacuated(dve, 1)

            def ada(l):
                wait_all_evacuated(dve, G_AT[f"ada{l}"] + 2 * ADA_W)
                link(v.tensor_tensor(mod[l][:], mod[l][:], VT[:, V_ADA + 48 * l:V_ADA + 48 * l + 48].unsqueeze(2
                                     ).to_broadcast([128, 48, 2]), ALU.add))
                link(v.tensor_scalar_add(mod[l][:, 8:16, :], mod[l][:, 8:16, :], 1.0))
                v.tensor_scalar_add(mod[l][:, 32:40, :], mod[l][:, 32:40, :], 1.0).then_inc(mod_ready, 1)
                dve.wait_ge(mod_ready, l + 1)

            dve.wait_ge(filt_in, 144)
            v.scalar_tensor_tensor(out=dabs[:], in0=dabs[:], scalar=-1.0, in1=dabs[:], op0=ALU.mult, op1=ALU.max).then_inc(dabs_ready, 1)
            ada(0)

            two_pi = 2.0 * math.pi
            c1 = float(np.float32(6.28125))
            c2 = float(np.round((two_pi - c1) * 2 ** 20) / 2 ** 20)
            c3 = float(np.float32(two_pi - c1 - c2))
            magic = float(1.5 * 2 ** 23)
            for n in range(2):
                g = G_AT["mlp"] + n
                wait_group(dve, g)
                v.tensor_scalar(marg[:], ps[g % 8][0:FH, 0:TOK], fcol[:, n:n + 1], fcol[:, 2:3], ALU.add, ALU.mult
                                ).then_inc(evacuated[g % 8], 1)
                wait_evacuated(dve, g)
                link(v.tensor_scalar(mrnd[:], marg[:], 1.0 / two_pi, magic, ALU.mult, ALU.add))
                link(v.tensor_scalar_add(mrnd[:], mrnd[:], -magic))
                for c in (c1, c2, c3):
                    link(v.scalar_tensor_tensor(out=marg[:], in0=mrnd[:], scalar=-c, in1=marg[:], op0=ALU.mult, op1=ALU.add))
                v.tensor_scalar(marg[:], marg[:], 3.1415925, -3.1415925, ALU.min, ALU.max).then_inc(marg_ready, 1)

            for t in range(TT):
                dve.wait_ge(decay_ready, t + 1)
                for h in range(2):
                    hs = slice(h * 512, (h + 1) * 512)
                    g = G_AT["filt"] + 4 * t + 2 * h
                    for d in range(2):
                        wait_group(dve, g + d)
                        v.tensor_tensor(ftmp[:, d, :], ps[(g + d) % 8][:, :],
                                        decay[:, t, d * D + h * 512:d * D + (h + 1) * 512], ALU.mult
                                        ).then_inc(evacuated[(g + d) % 8], 1)
                    wait_evacuated(dve, g)
                    wait_evacuated(dve, g + 1)
                    link(v.scalar_tensor_tensor(out=hsum[:, t, hs], in0=ftmp[:, 1, :], scalar=cols[:, 3 + t:4 + t],
                                                in1=ftmp[:, 0, :], op0=ALU.mult, op1=ALU.add))
                    link(v.tensor_tensor(hdif[:, t, hs], ftmp[:, 0, :], ftmp[:, 1, :], ALU.subtract))
            dve.wait_ge(dft_in, 48)
            skip = tmp[0:1, :, :].rearrange("p a n -> p (a n)")
            link(v.tensor_tensor(hsum[0:1, 0, :], hsum[0:1, 0, :], skip, ALU.add))
            v.tensor_tensor(hsum[0:1, 1, :], hsum[0:1, 1, :], skip, ALU.add).then_inc(taps_ready, 1)
            dve.wait_ge(taps_ready, 1)

            def gates(name):
                for n in range(4):
                    g = G_AT[name] + n
                    wait_group(dve, g)
                    v.tensor_copy(gate[:, n // 2, (n % 2) * 512:(n % 2 + 1) * 512], ps[g % 8][:, :]).then_inc(evacuated[g % 8], 1)

            def modulate_even(name, l, shift, scale):
                for j in range(0, KT, 2):
                    g = G_AT[name] + j
                    wait_group(dve, g)
                    for c, (a, b) in enumerate(((0, PROMPT), (PROMPT, TOK))):
                        last = v.tensor_scalar(hT[:, j, a:b], ps[g % 8][:, a:b], mod[l][:, scale + j, c:c + 1],
                                               mod[l][:, shift + j, c:c + 1], ALU.mult, ALU.add)
                    last.then_inc(evacuated[g % 8], 1)

            dve.wait_ge(zeros_out, 16)
            gates("gm0")
            link(v.memset(zt[:], 0.0))
            v.memset(acc[:], 0.0).then_inc(guards_ready, 1)
            dve.wait_ge(guards_ready, 1)
            modulate_even("xm0", 0, 0, 8)

            for n in range(24):
                g = G_AT["in"] + n
                part, j = divmod(n, KT)
                wait_evacuated(dve, g)
                z, a = zt[:, n % 2, :], acc[:, n % 2, :]
                W = PAD - 2
                tap = [VT[:, V_CW + 24 * i + n:V_CW + 24 * i + n + 1] for i in range(3)]
                link(v.tensor_scalar(a[:, 1:1 + W], z[:, 1:1 + W], tap[1], VT[:, V_CB + n:V_CB + n + 1], ALU.mult, ALU.add))
                link(v.scalar_tensor_tensor(out=a[:, 1:1 + W], in0=z[:, 0:W], scalar=tap[0], in1=a[:, 1:1 + W],
                                            op0=ALU.mult, op1=ALU.add))
                dst = (x0T[:, j, 1:1 + W], uT[:, j, 1:1 + W], a[:, 1:1 + W])[part]
                v.scalar_tensor_tensor(out=dst, in0=z[:, 2:2 + W], scalar=tap[2], in1=a[:, 1:1 + W],
                                       op0=ALU.mult, op1=ALU.add).then_inc(z_used, 1)
                dve.wait_ge(z_used, n + 1)
                if part == 2:
                    ins = v.tensor_tensor(uT[:, j, 1:1 + W], uT[:, j, 1:1 + W], a[:, 1:1 + W], ALU.mult)
                    if j == KT - 1:
                        ins.then_inc(u_ready, 1)
                    else:
                        link(ins)
            for n in range(6):
                q, h = divmod(n, 2)
                hs = slice(h * 512, (h + 1) * 512)
                gc = G_AT["dft"] + 2 * n
                wait_group(dve, gc)
                wait_group(dve, gc + 1)
                uc, us = ps[gc % 8], ps[(gc + 1) % 8]
                link(v.tensor_tensor(Y[:, q, 0, hs], uc[:, :], K[:, q, 0, hs], ALU.mult))
                v.tensor_tensor(Y[:, q, 1, hs], uc[:, :], K[:, q, 1, hs], ALU.mult).then_inc(evacuated[gc % 8], 1)
                link(v.tensor_tensor(tmp[:, 0, :], us[:, :], K[:, q, 1, hs], ALU.mult))
                v.tensor_tensor(tmp[:, 1, :], us[:, :], K[:, q, 0, hs], ALU.mult).then_inc(evacuated[(gc + 1) % 8], 1)
                wait_evacuated(dve, gc)
                wait_evacuated(dve, gc + 1)
                link(v.tensor_tensor(Y[:, q, 0, hs], Y[:, q, 0, hs], tmp[:, 0, :], ALU.subtract))
                v.tensor_tensor(Y[:, q, 1, hs], Y[:, q, 1, hs], tmp[:, 1, :], ALU.add).then_inc(Y_ready, 1)
                dve.wait_ge(Y_ready, n + 1)
            for j in range(KT):
                g = G_AT["inv"] + j
                wait_group(dve, g)
                for a, b, at_ in SEQ_AT:
                    last = v.tensor_tensor(yT[:, j, a:b], ps[g % 8][:, a:b], x0T[:, j, at_:at_ + b - a], ALU.mult)
                last.then_inc(evacuated[g % 8], 1)

            def layer_norm(n):
                for t in range(TT):
                    for h in range(2):
                        link(v.bn_stats(st[:, t, h, :], x[:, t, h * 512:(h + 1) * 512]))
                    link(v.bn_aggr(mv[:, t, :], st[:, t, :, :].rearrange("p a b -> p (a b)")))
                v.tensor_scalar_add(sd[:, 1, :], mv[:, :, 1], LN_EPS).then_inc(var_ready, 1)
                dve.wait_ge(sd_ready, n + 1)
                link(v.reciprocal(sd[:, 0, :], sd[:, 0, :]))
                for t in range(TT):
                    link(v.tensor_scalar(x[:, t, :], x[:, t, :], mv[:, t, 0:1], sd[:, 0, t:t + 1], ALU.subtract, ALU.mult))
                for t in range(TT):
                    link(v.tensor_tensor(x[:, t, :], x[:, t, :], rows[:, 1, :], ALU.mult))
                for t in range(TT):
                    ins = v.tensor_tensor(x[:, t, :], x[:, t, :], rows[:, 2, :], ALU.add)
                    if t < TT - 1:
                        link(ins)
                ins.then_inc(ln_done, 1)
                dve.wait_ge(ln_done, n + 1)

            def residual(l):
                dve.wait_ge(rows_in, 80 * l + 48)
                if l == 0:
                    dve.wait_ge(x_in, 32)
                for n in range(6):
                    g = G_AT[f"out{l}"] + n
                    h, t = divmod(n, TT)
                    hs = slice(h * 512, (h + 1) * 512)
                    wait_group(dve, g)
                    buf = tmp[:, n % 2, :]
                    v.tensor_tensor(buf, ps[g % 8][:, :], rows[:, 0, hs], ALU.add).then_inc(evacuated[g % 8], 1)
                    wait_evacuated(dve, g)
                    link(v.tensor_tensor(buf, buf, gate[:, COND[t], hs], ALU.mult))
                    link(v.scalar_tensor_tensor(out=x[:, t, hs], in0=x[:, t, hs], scalar=ALPHA, in1=buf,
                                                op0=ALU.mult, op1=ALU.add))

            def first_of(dst, src, top):
                link(v.tensor_tensor(sc4[:], src, top.unsqueeze(2).to_broadcast([128, TT, 4]), ALU.is_equal))
                link(v.tensor_tensor(sc4[:], sc4[:], mc[:, MC_PREF:MC_PREF + 4].unsqueeze(1).to_broadcast([128, TT, 4]), ALU.mult))
                link(v.reduce_max(mx[:, 7, :], sc4[:], AX))
                link(v.tensor_tensor(dst, sc4[:], mx[:, 7, :].unsqueeze(2).to_broadcast([128, TT, 4]), ALU.is_equal))

            def moe(l):
                S = moe_sems[l]
                gates(f"gf{l}")
                modulate_even(f"xf{l}", l, 24, 32)
                g = G_AT[f"logit{l}"]
                wait_group(dve, g)
                dve.wait_ge(moe_in, 80 * (l + 1))
                v.tensor_tensor(Lg[:], ps[g % 8][:, 0:60].rearrange("p (t n) -> p t n", t=TT),
                                br[:].unsqueeze(1).to_broadcast([128, TT, 20]), ALU.add).then_inc(evacuated[g % 8], 1)
                wait_evacuated(dve, g)
                gl = Lg[:, :, 0:4]
                link(v.reduce_max(mx[:, 0, :], gl, AX))
                first_of(ohg[:], gl, mx[:, 0, :])
                pick = t256[:, 0:48].rearrange("p (t g j) -> p t g j", t=TT, g=4)
                link(v.tensor_tensor(pick, Lg[:, :, 4:20].rearrange("p t (g j) -> p t g j", g=4),
                                     ohg[:].unsqueeze(3).to_broadcast([128, TT, 4, 4]), ALU.mult))
                link(v.tensor_reduce(esel[:], pick.rearrange("p t g j -> p t j g"), AX, ALU.add))
                link(v.reduce_max(mx[:, 1, :], esel[:], AX))
                first_of(o1[:], esel[:], mx[:, 1, :])
                link(v.scalar_tensor_tensor(out=esel[:], in0=o1[:], scalar=NEG, in1=esel[:], op0=ALU.mult, op1=ALU.add))
                link(v.reduce_max(mx[:, 2, :], esel[:], AX))
                first_of(o2[:], esel[:], mx[:, 2, :])
                m4 = [m[:].rearrange("p t (g j) -> p t g j", g=4) for m in (M1, M2)]
                for m, oh in zip(m4, (o1, o2)):
                    link(v.tensor_tensor(m, ohg[:].unsqueeze(3).to_broadcast([128, TT, 4, 4]),
                                         oh[:].unsqueeze(2).to_broadcast([128, TT, 4, 4]), ALU.mult))
                v.tensor_tensor(Msel[:], M1[:], M2[:], ALU.add).then_inc(M_ready, 1)
                dve.wait_ge(M_ready, l + 1)
                link(v.tensor_tensor(ex[:, 0:12].rearrange("p (t g) -> p t g", t=TT), gl,
                                     mx[:, 0, :].unsqueeze(2).to_broadcast([128, TT, 4]), ALU.subtract))
                v.tensor_tensor(ex[:, 12:15], mx[:, 2, :], mx[:, 1, :], ALU.subtract).then_inc(ex_ready, 1)
                g = G_AT[f"rank{l}"]
                wait_group(dve, g)
                v.tensor_copy(R[:], ps[g % 8][:, 0:64]).then_inc(evacuated[g % 8], 1)
                wait_evacuated(dve, g)
                rk, cnt = R[:, 0:48].rearrange("p (t e) -> p t e", t=TT), R[:, 48:64]
                over = t256[:, 0:16 * MAX_NB].rearrange("p (e j) -> p e j", j=MAX_NB)
                link(v.tensor_tensor(over, cnt.unsqueeze(2).to_broadcast([128, 16, MAX_NB]),
                                     mc[:, MC_THR:MC_THR + MAX_NB].unsqueeze(1).to_broadcast([128, 16, MAX_NB]), ALU.is_gt))
                link(v.tensor_reduce(nbase[:, 0:16], over, AX, ALU.add))
                link(v.tensor_scalar_max(nbase[:, 0:16], nbase[:, 0:16], 1.0))
                before = t256[:, :].rearrange("p (e j) -> p e j", j=16)
                link(v.tensor_tensor(before, nbase[:, 0:16].unsqueeze(1).to_broadcast([128, 16, 16]),
                                     mc[:, MC_BEFORE:MC_BEFORE + 256].rearrange("p (e j) -> p e j", j=16), ALU.mult))
                link(v.tensor_reduce(nbase[:, 16:32], before, AX, ALU.add))
                link(v.tensor_tensor(nbase[:, 32:33], nbase[:, 15:16], nbase[:, 31:32], ALU.add))
                v.tensor_copy(NBi[:], nbase[:]).then_inc(nb_ready, 1)
                dve.wait_ge(nb_ready, l + 1)
                link(v.scalar_tensor_tensor(out=pos[:], in0=nbase[:, 16:32].unsqueeze(1).to_broadcast([128, TT, 16]),
                                            scalar=float(SLOT_TOK), in1=rk, op0=ALU.mult, op1=ALU.add))
                for k, m in enumerate((M1, M2)):
                    link(v.tensor_tensor(t48[:], m[:], pos[:], ALU.mult))
                    link(v.tensor_reduce(idxf[:, k, :], t48[:], AX, ALU.add))
                v.tensor_copy(idx[:], idxf[:]).then_inc(idx_ready, 1)
                dve.wait_ge(ex_done, l + 1)
                link(v.tensor_reduce(mx[:, 3, :], ex[:, 0:12].rearrange("p (t g) -> p t g", t=TT), AX, ALU.add))
                link(v.tensor_scalar_add(mx[:, 4, :], ex[:, 12:15], 1.0))
                link(v.tensor_tensor(mx[:, 3, :], mx[:, 3, :], mx[:, 4, :], ALU.mult))
                link(v.reciprocal(wk[:, 0, :], mx[:, 3, :]))
                link(v.tensor_tensor(wk[:, 1, :], wk[:, 0, :], ex[:, 12:15], ALU.mult))
                v.memset(credit[:, 2:3], 0.0).then_inc(S["y_stored"], 16)
                total = dve.value_load(NBi[0:1, 32:33], min_val=EXPERTS, max_val=MAX_BLOCKS)

                def flipped(n):
                    dve.wait_ge(S["flip_ready"], n)
                    v.tensor_copy(xg[:, 0:4, :].rearrange("p k s -> p (k s)"), ps[0][:, :]).then_inc(S["xg_ready"], 1)

                flipped(1)
                with dve.Fori(0, total) as b:
                    dve.wait_ge(S["b_ready"], b + 1)
                    dve.wait_ge(S["sa_ready"], b + 1)
                    v.tensor_tensor(he[:].rearrange("p f s -> p (f s)"), sa[:].rearrange("p f s -> p (f s)"),
                                    ps[2][:, 0:4 * SLOT_TOK], ALU.mult).then_inc(S["he_ready"], 1)
                    flipped(b + 2)
                    dve.wait_ge(S["y0_ready"], b + 1)
                    dve.wait_ge(S["y_stored"], b * 16 + 16)
                    v.tensor_copy(ysb[:, 0:512], ps[3][0:SLOT_TOK, :]).then_inc(S["ysb0_ready"], 1)
                v.memset(credit[:, 5:6], 0.0).then_inc(blocks_done, 1)
                dve.wait_ge(S["rows_back"], 96)
                for t in range(TT):
                    link(v.tensor_scalar(gath[:, 0, t, :], gath[:, 0, t, :], wk[:, 0, t:t + 1], None, ALU.mult))
                for t in range(TT):
                    link(v.scalar_tensor_tensor(out=gath[:, 0, t, :], in0=gath[:, 1, t, :], scalar=wk[:, 1, t:t + 1],
                                                in1=gath[:, 0, t, :], op0=ALU.mult, op1=ALU.add))
                for t in range(TT):
                    link(v.tensor_tensor(gath[:, 0, t, :], gath[:, 0, t, :], gate[:, COND[t], :], ALU.mult))
                for t in range(TT):
                    link(v.scalar_tensor_tensor(out=x[:, t, :], in0=x[:, t, :], scalar=ALPHA, in1=gath[:, 0, t, :],
                                                op0=ALU.mult, op1=ALU.add))
                dve.wait_ge(rows_in, 80 * (l + 1))
                layer_norm(2 * l + 1)

            residual(0)
            layer_norm(0)
            moe(0)

            ada(1)
            gates("gm1")
            modulate_even("xm1", 1, 0, 8)
            for j in range(KT):
                g = G_AT["qk"] + j
                wait_group(dve, g)
                v.tensor_scalar(qT[:, j, :], ps[g % 8][:, 0:TOK], VT[:, V_BQK + j:V_BQK + j + 1], DH ** -0.5,
                                ALU.add, ALU.mult).then_inc(evacuated[g % 8], 1)
            dve.wait_ge(att_in, 80)
            for n in range(6):
                g = G_AT["v"] + n
                h, t = divmod(n, TT)
                hs = slice(h * 512, (h + 1) * 512)
                wait_group(dve, g)
                v.tensor_tensor(tok[:, t, hs], ps[g % 8][:, :], bv[:, hs], ALU.add).then_inc(evacuated[g % 8], 1)

            units = TT * HEADS

            def maximum(u):
                dve.wait_ge(s_ready, u + 1)
                s = ps[u % 3]
                n = 128
                if u >= HEADS:
                    m = u - HEADS
                    dve.wait_ge(bm_ready, m + 1)
                    link(v.tensor_tensor(s[:, 0:256], s[:, 0:256], bm[:, m % 4, :], ALU.add))
                    n = 384
                v.reduce_max(nmax[:, u:u + 1], s[:, 0:n], AX, negate=True).then_inc(max_ready, 1)

            def heads_out(o):
                dve.wait_ge(p_ready, 8 * o + 8)
                link(v.reciprocal(rden[:, 8 * o:8 * o + 8], den[:, 8 * o:8 * o + 8]))
                dve.wait_ge(pv_done, 8 * o + 8)
                t, h = divmod(o, 2)
                v.tensor_tensor(otok[:, t, h * 512:(h + 1) * 512].rearrange("p (h d) -> p h d", d=DH),
                                ps[5 + o % 3][:, :].rearrange("p (h d) -> p h d", d=DH),
                                rden[:, 8 * o:8 * o + 8].unsqueeze(2).to_broadcast([128, 8, DH]), ALU.mult
                                ).then_inc(o_evac, 1)

            for n in range(units + 5):
                if n < units:
                    maximum(n)
                if n >= 12 and (n - 12) % 8 == 0:
                    heads_out((n - 12) // 8)
            for j in range(KT):
                g = G_AT["ot"] + j
                wait_group(dve, g)
                v.tensor_copy(oT[:, j, :], ps[g % 8][:, 0:TOK]).then_inc(evacuated[g % 8], 1)
            residual(1)
            layer_norm(2)
            moe(1)


_INS = ["x_prompt", "x_sample", "cache_k", "cache_v", "c", "c_ctx", "w_ada", "b_ada", "ln_g", "ln_b",
        "hy_w_in", "hy_b_in", "hy_conv_w", "hy_conv_b", "hy_f_w1", "hy_f_b1", "hy_f_w2", "hy_f_b2", "hy_f_w3",
        "hy_f_freq", "hy_decay", "hy_d", "hy_w_out", "hy_b_out",
        "na_w_qkv", "na_b_qkv", "na_rpb", "na_w_out", "na_b_out",
        "moe_w_group", "moe_b_group", "moe_w_expert", "moe_b_expert", "moe_w_up", "moe_w_down"]
_OUTS = [("y_prompt", (1, PROMPT, D)), ("y_sample", (1, SAMPLE, D)),
         ("new_k", (1, 1, HEADS, PROMPT, DH)), ("new_v", (1, 1, HEADS, PROMPT, DH))]


def kernel(**inputs):
    import concourse.bacc as _bacc
    from concourse.bass_utils import run_bass_kernel_spmd as _run

    nc = _bacc.Bacc("TRN2", target_bir_lowering=False, num_devices=1)
    arrays = {n: np.ascontiguousarray(inputs[n]) for n in _INS}
    arrays["na_rpb_rev"] = np.ascontiguousarray(arrays.pop("na_rpb").reshape(HEADS, RPB_H)[:, ::-1])
    arrays.update(shape_constants())
    aps = {n: nc.dram_tensor(f"in_{n}", a.shape, mybir.dt.from_np(a.dtype), kind="ExternalInput").ap()
           for n, a in arrays.items()}
    outs = [nc.dram_tensor(f"out_{n}", s, mybir.dt.float32, kind="ExternalOutput").ap() for n, s in _OUTS]
    build(nc, aps, *outs)
    r = _run(nc, [{f"in_{n}": a for n, a in arrays.items()}], core_ids=[0])
    return tuple(r.results[0][f"out_{n}"] for n, _ in _OUTS)
```

```python
import math
from contextlib import ExitStack

import numpy as np
import concourse.bass as bass
from concourse import mybir

D = 1024
KT = D // 128
PROMPT, SAMPLE = 128, 256
TOK = PROMPT + SAMPLE
TT = TOK // 128
COND = [0, 1, 1]
DEPTH = 2
HEADS, DH = 16, 64
PAST = 128
GRID_W, ROWS, WIN_ROWS, WIN_COLS = 64, SAMPLE // 64, 8, 16
RPB_C = 2 * WIN_COLS - 1
RPB_H = (2 * WIN_ROWS - 1) * RPB_C
RPB_WIN = 5 * RPB_C + GRID_W
EXPERTS, GROUPS, PER_GROUP = 16, 4, 4
FE = 512
SLOT_TOK = 128
MAX_NB = TOK // SLOT_TOK
MAX_BLOCKS = 2 * TOK // SLOT_TOK + EXPERTS
FH, FEAT = 64, 33
ALPHA = (2 * DEPTH) ** 0.25
LN_EPS = 1e-5
PAD = TOK + 3
SEQ_AT = [(0, PROMPT, 1), (PROMPT, TOK, PROMPT + 2)]
TILE_AT = [1, PROMPT + 2, PROMPT + 2 + 128]
NEG = -1.0e30

RING = 6
ADA_EARLY = 6
ADA_W, IN_W, OUT_W, QKV_W = 12, 6, 2, 6
MOE_W = 3 * EXPERTS
W_AT, W_N = {}, {}
_at = 0
for _name, _n in [("ada0", ADA_W), ("in", IN_W), ("out0", OUT_W), ("ada1", ADA_EARLY), ("moe0", MOE_W),
                  ("ada1late", ADA_W - ADA_EARLY), ("qkv", QKV_W), ("out1", OUT_W), ("moe1", MOE_W)]:
    W_AT[_name], W_N[_name] = _at, _n
    _at += _n

G_AT = {}
_at = 0
for _name, _n in [("vec", 2), ("ada0a", 6), ("mlp0", 1), ("ada0b", 4), ("mlp1", 1),
                  ("ada0c", 4), ("filt", 12), ("ada0d", 10), ("filtK", 12), ("gm0", 4), ("xm0", 8),
                  ("in", 24), ("ut", 6), ("dft", 12), ("inv", 8), ("out0", 6), ("ada1a", 4), ("gf0", 4), ("xf0", 8),
                  ("logit0", 1), ("ada1b", 4), ("rank0", 1), ("tok0", 6), ("ada1c", 4), ("ada1d", 12),
                  ("gm1", 4), ("xm1", 8), ("qk", 16), ("v", 6), ("kout", 2), ("kctx", 2),
                  ("ot", 8), ("out1", 6), ("gf1", 4), ("xf1", 8), ("logit1", 1), ("rank1", 1), ("tok1", 6)]:
    G_AT[_name] = _at
    _at += _n

ADA_SEG = {0: [("ada0a", 0, 3), ("ada0b", 3, 2), ("ada0c", 5, 2), ("ada0d", 7, 5)],
           1: [("ada1a", 0, 2), ("ada1b", 2, 2), ("ada1c", 4, 2), ("ada1d", ADA_EARLY, 6)]}


def ada_piece(l, n):
    return W_AT["ada1late"] + n - ADA_EARLY if l == 1 and n >= ADA_EARLY else W_AT[f"ada{l}"] + n


def ada_row(n):
    return 0 if n == 0 else 2 * n - 1


def ada_col(n, count):
    return min(2 * n + 2, 2 * count - 1)


V_ADA, V_CC, V_CS, V_BQK = 0, 96, 104, 112
V_BIN, V_CW, V_CB = 128, 152, 224
DFT_COLS = 2560
MC_TRI, MC_ONES, MC_BEFORE, MC_THR = 0, 128, 256, 512
MC_PREF = MC_THR + MAX_NB
MC_COLS = MC_PREF + 4


def shape_constants():
    def tables(L):
        w = 2 * np.pi * (np.arange(L) + 0.5) / (2 * L)
        a = np.outer(np.arange(L), w)
        return np.cos(a), np.sin(a)

    def tiles(m):
        return m.reshape(m.shape[0] // 128, 128, m.shape[1]).transpose(1, 0, 2).reshape(128, -1)

    cs, ss = tables(SAMPLE)
    cp, sp = tables(PROMPT)
    dft = np.concatenate([tiles(cs), tiles(ss), tiles(cs.T / SAMPLE), tiles(ss.T / SAMPLE),
                          cp, sp, cp.T / PROMPT, sp.T / PROMPT], axis=1).astype(np.float32)
    feats, ts = [], []
    for L in (PROMPT, SAMPLE):
        pos = np.arange(L, dtype=np.float32)[:, None]
        t = pos / np.float32(L - 1)
        bands = np.linspace(1e-4, 15, 16, dtype=np.float32)
        ang = np.float32(2.0 * math.pi / L) * pos * bands
        feats.append(np.concatenate([t, np.cos(ang), -np.sin(ang)], axis=-1))
        ts.append(t[:, 0])
    feat = np.concatenate(feats).T.astype(np.float32)
    cols = np.zeros((128, 8), np.float32)
    cols[:, 0:3] = -np.concatenate(ts).reshape(3, 128).T
    cols[:, 3:6] = 1.0
    cols[0, 3] = cols[0, 4] = 0.0
    col = np.arange(GRID_W)
    start = np.clip(col - WIN_COLS // 2, 0, GRID_W - WIN_COLS)
    band = (col[None] >= start[:, None]) & (col[None] < start[:, None] + WIN_COLS)
    band = np.tile(np.where(band, 0.0, NEG), (2, 1)).astype(np.float32)
    moe = np.zeros((128, MC_COLS), np.float32)
    moe[:, MC_TRI:MC_TRI + 128] = np.triu(np.ones((128, 128)), 1)
    moe[:, MC_ONES:MC_ONES + 128] = 1.0
    moe[:, MC_BEFORE:MC_BEFORE + 256] = np.tril(np.ones((16, 16)), -1).reshape(-1)
    moe[:, MC_THR:MC_THR + MAX_NB] = np.arange(MAX_NB) * SLOT_TOK
    moe[:, MC_PREF:MC_PREF + 4] = [4, 3, 2, 1]
    return {"k_ident": np.eye(128, dtype=np.float32), "k_dft": dft, "k_feat": feat, "k_cols": cols,
            "k_band": band, "k_moe": moe}


def build(nc, A, y_prompt, y_sample, new_k, new_v):
    f32, i32 = mybir.dt.float32, mybir.dt.int32
    ACT = mybir.ActivationFunctionType
    ALU = mybir.AluOpType
    AX = mybir.AxisListType.X

    ctx = ExitStack()
    with ctx:
        origin = (nc.sbuf_base + 31) // 32 * 32

        def at(name, shape, offset, dt=f32):
            return nc.alloc_sbuf_tensor_at(name, shape, dt, offset=origin + offset)

        RA = RING * 16384
        RX0 = RA + 12288 + 12384
        RTOK = RX0 + 12384
        RK = RTOK + 12288
        RM = RK + 24576
        RS = RM + 15872
        ring = [at(f"ring{r}", [128, 4096], r * 16384) for r in range(RING)]
        hT = at("hT", [128, KT, TOK], RA)
        uT = at("uT", [128, KT, PAD], RA + 12288)
        hsum = at("hsum", [128, 3, D], RA)
        hdif = at("hdif", [128, 3, D], RA + 12288)
        feat = at("feat", [FEAT, TOK], RA)
        marg = at("marg", [FH, TOK], RA + 1536)
        mrnd = at("mrnd", [FH, TOK], RA + 3072)
        mh1 = at("mh1", [FH, TOK], RA + 4608)
        fw1 = at("fw1", [FEAT, FH], RA + 6144)
        fw2 = at("fw2", [FH, FH], RA + 6400)
        Y = at("Y", [128, 3, 2, D], RA)
        otok = at("otok", [128, TT, D], RA)
        kT = at("kT", [128, KT, TOK], RA + 12288)
        gath = at("gath", [128, 2, TT, D], RA)
        x0T = at("x0T", [128, KT, PAD], RX0)
        dabs = at("dabs", [128, 2 * D], RX0)
        mh2 = at("mh2", [FH, TOK], RX0 + 8192)
        V1 = at("V1", [128, 128], RX0 + 9728)
        V2 = at("V2", [128, 128], RX0 + 10240)
        qT = at("qT", [128, KT, TOK], RX0)
        oT = at("oT", [128, KT, TOK], RX0)
        mc = at("mc", [128, MC_COLS], RX0)
        tok = at("tok", [128, TT, D], RTOK)
        fw3 = at("fw3", [FH, 2 * D], RTOK)
        ftmp = at("ftmp", [128, 2, 512], RTOK + 8192)
        zt = at("zt", [128, 2, PAD + 1], RTOK)
        acc = at("acc", [128, 2, PAD + 1], RTOK + 2 * (PAD + 1) * 4)
        yT = at("yT", [128, KT, TOK], RTOK)
        decay = at("decay", [128, 3, 2 * D], RK)
        K = at("K", [128, 3, 2, D], RK)
        rows = at("rows", [128, 3, D], RK)
        rpb = at("rpb", [128, HEADS, RPB_WIN], RK)
        bm = at("bm", [128, 4, 256], RK + 14336)
        kraw = at("kraw", [128, D], RK + 18432)
        dft = at("dft", [128, DFT_COLS], RM)
        tmp = at("tmp", [128, 2, 512], RM + 10240)
        vctx = at("vctx", [128, D], RM)
        kctxT = at("kctxT", [128, KT, 128], RM + 4096)
        P = at("P", [128, 3, 384], RM + 8192)
        PT = at("PT", [128, 2, 384], RM + 12800)
        bv = at("bv", [128, D], RM + 8192)
        kst = at("kst", [128, D], RK + 20480)
        wr = at("wr", [128, KT, 20], RM)
        br = at("br", [128, 20], RM + 640)
        Lg = at("Lg", [128, TT, 20], RM + 768)
        ohg = at("ohg", [128, TT, 4], RM + 1024)
        o1 = at("o1", [128, TT, 4], RM + 1088)
        o2 = at("o2", [128, TT, 4], RM + 1152)
        esel = at("esel", [128, TT, 4], RM + 1216)
        sc4 = at("sc4", [128, TT, 4], RM + 1280)
        mx = at("mx", [128, 8, TT], RM + 1344)
        ex = at("ex", [128, 15], RM + 1472)
        M1 = at("M1", [128, TT, 16], RM + 1536)
        M2 = at("M2", [128, TT, 16], RM + 1728)
        Msel = at("Msel", [128, TT, 16], RM + 1920)
        R = at("R", [128, 64], RM + 2112)
        t48 = at("t48", [128, TT, 16], RM + 2560)
        nbase = at("nbase", [128, 33], RM + 2752)
        t256 = at("t256", [128, 256], RM + 2912)
        NBi = at("NBi", [128, 33], RM + 3936, i32)
        idxf = at("idxf", [128, 2, TT], RM + 4096)
        idx = at("idx", [128, 2, TT], RM + 4128, i32)
        pos = at("pos", [128, TT, 16], RM + 4160)
        wk = at("wk", [128, 2, TT], RM + 4352)
        xg = at("xg", [128, KT, SLOT_TOK], RM + 5888)
        sa = at("sa", [128, 4, SLOT_TOK], RM + 9984)
        he = at("he", [128, 4, SLOT_TOK], RM + 12032)
        xraw = at("xraw", [SLOT_TOK, D], RK + 12288)
        ysb = at("ysb", [SLOT_TOK, D], RK + 16384)
        arow_at = {0: at("arow0", [2, 2, 512], RS + 12288 + 4096), 1: at("arow1", [2, 2, 512], RA + 12288),
                   2: at("arow2", [2, 2, 512], RX0)}

        def arow(l, seg):
            return arow_at[l + (l == 1 and seg == 3)]
        o = RS
        x = at("x", [128, TT, D], o); o += 12288
        gate = at("gate", [128, 2, D], o); o += 8192
        ident = at("ident", [128, 128], o); o += 512
        VT = at("VT", [128, 248], o); o += 992
        mod = [at(f"mod{l}", [128, 48, 2], o + 384 * l) for l in range(2)]; o += 768
        scond = at("scond", [128, KT, 2], o); o += 64
        cols = at("cols", [128, 8], o); o += 32
        band = at("band", [128, GRID_W], o); o += 256
        fcol = at("fcol", [FH, 4], o); o += 32
        st = at("st", [128, TT, 2, 6], o); o += 160
        mv = at("mv", [128, TT, 2], o); o += 32
        sd = at("sd", [128, 3, TT], o); o += 64
        nmax = at("nmax", [128, 48], o); o += 192
        den = at("den", [128, 48], o); o += 192
        rden = at("rden", [128, 48], o); o += 192
        credit = at("credit", [128, 8], o); o += 32
        assert origin + o <= nc.sbuf_usable_end, (origin + o, nc.sbuf_usable_end)

        ps = [ctx.enter_context(nc.psum_tensor(f"bank{i}", [128, 512], f32)) for i in range(8)]
        slots = nc.dram_tensor("slots", [(MAX_BLOCKS + 2) * SLOT_TOK, D], f32).ap()

        def sem(name):
            return ctx.enter_context(nc.semaphore(name))

        w_loaded = [sem(f"w_loaded{r}") for r in range(RING)]
        expert_done = [sem(f"expert_done{l}") for l in range(DEPTH)]
        group_ready = sem("group_ready")
        evacuated = [sem(f"evacuated{b}") for b in range(8)]
        first_in, x_in, filt_in, rows_in, moe_in, att_in, dft_in = (
            sem(n) for n in ("first_in", "x_in", "filt_in", "rows_in", "moe_in", "att_in", "dft_in"))
        scond_ready, mod_ready, cond_cols = sem("scond_ready"), sem("mod_ready"), sem("cond_cols")
        marg_ready, mh_ready, decay_ready, taps_ready = (
            sem(n) for n in ("marg_ready", "mh_ready", "decay_ready", "taps_ready"))
        dabs_ready, guards_ready, z_ready, z_used, u_ready, Y_ready = (
            sem(n) for n in ("dabs_ready", "guards_ready", "z_ready", "z_used", "u_ready", "Y_ready"))
        var_ready, sd_ready, mean_ready, norm_done, ln_done, dve_step, first_scaled = (
            sem(n) for n in ("var_ready", "sd_ready", "mean_ready", "norm_done", "ln_done", "dve_step", "first_scaled"))
        ex_ready, ex_done, M_ready, nb_ready, idx_ready = (
            sem(n) for n in ("ex_ready", "ex_done", "M_ready", "nb_ready", "idx_ready"))
        s_ready, max_ready, p_ready, t_ready, pt_ready, pv_done, o_evac, bm_ready = (
            sem(n) for n in ("s_ready", "max_ready", "p_ready", "t_ready", "pt_ready", "pv_done", "o_evac", "bm_ready"))
        kv_out = sem("kv_out")
        zero_ready, zeros_out = sem("zero_ready"), sem("zeros_out")
        all_stored = sem("all_stored")
        blocks_done = sem("blocks_done")
        y_out = sem("y_out")
        moe_sems = []
        for l in range(DEPTH):
            moe_sems.append({n: sem(f"{n}{l}") for n in (
                "slots_filled", "xraw0_in", "xraw_in", "flip_ready", "xg_ready", "a_ready", "sa_ready", "b_ready", "he_ready",
                "y0_ready", "y1_ready", "ysb0_ready", "ysb1_ready", "y_stored", "rows_back0_", "rows_back1_", "rows_back2_")})

        block = ctx.enter_context(nc.Block())

        def w_view(i, k, n):
            return ring[i % RING][:, :].rearrange("p (k n) -> p k n", k=k)

        def wait_weights(eng, i):
            eng.wait_ge(w_loaded[i % RING], 16 * (i // RING + 1))

        def wait_group(eng, g):
            eng.wait_ge(group_ready, g + 1)

        def wait_evacuated(eng, g):
            eng.wait_ge(evacuated[g % 8], g // 8 + 1)

        def wait_all_evacuated(eng, end):
            for g in range(end - 8, end):
                wait_evacuated(eng, g)

        @block.sync
        def _(sp):
            def last_group(j):
                for l in range(DEPTH):
                    for seg, first, count in ADA_SEG[l]:
                        for n in range(count):
                            if ada_piece(l, first + n) == j:
                                return G_AT[seg] + ada_row(n)
                    if 0 <= j - W_AT[f"out{l}"] < OUT_W:
                        return G_AT[f"out{l}"] + OUT_W * (TT - 1) + j - W_AT[f"out{l}"]
                for name, group, groups in (("in", "in", 4), ("qkv", "qk", 4)):
                    s = j - W_AT[name]
                    if 0 <= s < W_N[name]:
                        if name == "qkv" and s >= 4:
                            return G_AT["v"] + TT * (s - 4) + TT - 1
                        return G_AT[group] + groups * s + groups - 1

            def wait_slot_free(i):
                j = i - RING
                if j < 0:
                    return
                for l in range(DEPTH):
                    m = W_AT[f"moe{l}"]
                    if m <= j < m + MOE_W:
                        sp.wait_ge(expert_done[l], (j - m) // 3 + 1)
                        return
                sp.wait_ge(group_ready, last_group(j) + 1)

            def load(i, src, k):
                wait_slot_free(i)
                sp.dma_start(w_view(i, k, 4096 // k), src.rearrange("(k p) n -> p k n", p=128)
                             ).then_inc(w_loaded[i % RING], 16)

            def experts(l):
                up, down = A["moe_w_up"][l], A["moe_w_down"][l]
                first = W_AT[f"moe{l}"]

                def piece(i, src, k, n):
                    sp.dma_start(w_view(i, k, n), src.rearrange("o (k p) n -> p (o k) n", p=128)
                                 ).then_inc(w_loaded[i % RING], 16)

                def expert(e, i0, free):
                    for c in range(3):
                        free(c)
                        src = (up[bass.ds(e, 1), :, c * FE:(c + 1) * FE] if c < 2 else down[bass.ds(e, 1), :, :])
                        piece(i0 + c, src, 8 if c < 2 else 4, 512 if c < 2 else 1024)

                for e in range(2):
                    expert(e, first + 3 * e, lambda c, e=e: wait_slot_free(first + 3 * e + c))
                with sp.Fori(1, EXPERTS // 2) as p:
                    for half in range(2):
                        expert(2 * p + half, first + 3 * half,
                               lambda c, half=half: sp.wait_ge(expert_done[l], 2 * p + half - 1) if c == 0 else None)

            for s in range(ADA_W):
                if s == 1:
                    sp.wait_ge(first_in, 128)
                load(W_AT["ada0"] + s, A["w_ada"][0][:, s * 512:(s + 1) * 512], 8)
            for s in range(IN_W):
                load(W_AT["in"] + s, A["hy_w_in"][0][:, s * 512:(s + 1) * 512], 8)
            for s in range(OUT_W):
                load(W_AT["out0"] + s, A["hy_w_out"][0][:, s * 512:(s + 1) * 512], 8)
            for s in range(ADA_EARLY):
                load(ada_piece(1, s), A["w_ada"][1][:, s * 512:(s + 1) * 512], 8)
            experts(0)
            for s in range(ADA_EARLY, ADA_W):
                if s == ADA_EARLY + 4:
                    sp.wait_ge(moe_sems[0]["rows_back2_"], 32)
                load(ada_piece(1, s), A["w_ada"][1][:, s * 512:(s + 1) * 512], 8)
            for s in range(QKV_W):
                load(W_AT["qkv"] + s, A["na_w_qkv"][0][:, s * 512:(s + 1) * 512], 8)
            for s in range(OUT_W):
                load(W_AT["out1"] + s, A["na_w_out"][0][:, s * 512:(s + 1) * 512], 8)
            experts(1)
            for t in range(TT):
                sp.wait_ge(ln_done, 3 * TT + t + 1)
                dst = y_prompt[0] if t == 0 else y_sample[0, (t - 1) * 128:t * 128, :]
                sp.dma_start(dst, x[:, t, :]).then_inc(y_out, 16)
            sp.wait_ge(y_out, 48)

        @block.gpsimd
        def _(pool):
            def row_to_all(dst, src, n):
                return pool.dma_start(dst, bass.AP(src.tensor, src.offset, [[0, 128], [1, n]]))

            pool.dma_start(feat[:], A["k_feat"]).then_inc(filt_in, 16)
            pool.dma_start(fw1[:], A["hy_f_w1"][0]).then_inc(filt_in, 16)
            pool.dma_start(fw2[:], A["hy_f_w2"][0]).then_inc(filt_in, 16)
            pool.dma_start(fw3[:], A["hy_f_w3"][0]).then_inc(filt_in, 16)
            pool.dma_start(cols[:], A["k_cols"]).then_inc(filt_in, 16)
            for i, n in enumerate(("hy_f_b1", "hy_f_b2", "hy_f_freq")):
                pool.dma_start(fcol[:, i:i + 1], A[n].rearrange("a (p o) -> p (a o)", o=1)).then_inc(filt_in, 16)
            row_to_all(dabs[:], A["hy_decay"], 2 * D).then_inc(filt_in, 16)
            pool.dma_start(dft[:], A["k_dft"]).then_inc(dft_in, 16)
            pool.dma_start(band[:], A["k_band"]).then_inc(dft_in, 16)
            pool.dma_start(tmp[0:1, :, :].rearrange("p a n -> p (a n)"), A["hy_d"]).then_inc(dft_in, 16)

            pool.wait_ge(taps_ready, 1)
            nc.gpsimd.memset(tmp[:], 0.0).then_inc(zero_ready, 1)
            pool.wait_ge(zero_ready, 1)
            pool.dma_start(slots.rearrange("(a p) d -> p a d", p=128),
                           tmp[:].rearrange("p a n -> p (a n)").unsqueeze(1
                           ).to_broadcast([128, (MAX_BLOCKS + 2) * SLOT_TOK // 128, D])).then_inc(zeros_out, 16)

            def load_rows(l, which, bias):
                if bias is not None:
                    row_to_all(rows[:, 0, :], bias, D).then_inc(rows_in, 16)
                row_to_all(rows[:, 1, :], A["ln_g"][l, which], D).then_inc(rows_in, 16)
                row_to_all(rows[:, 2, :], A["ln_b"][l, which], D).then_inc(rows_in, 16)

            def moe_side(l):
                S = moe_sems[l]
                pool.wait_ge(ln_done, TT * (2 * l + 1))
                pool.dma_start(wr[:, :, 0:4], A["moe_w_group"][l].rearrange("(k p) n -> p k n", p=128)).then_inc(moe_in, 16)
                pool.dma_start(wr[:, :, 4:20], A["moe_w_expert"][l].rearrange("(k p) n -> p k n", p=128)).then_inc(moe_in, 16)
                row_to_all(br[:, 0:4], A["moe_b_group"][l], 4).then_inc(moe_in, 16)
                row_to_all(br[:, 4:20], A["moe_b_expert"][l], 16).then_inc(moe_in, 16)
                pool.dma_start(mc[:], A["k_moe"]).then_inc(moe_in, 16)
                load_rows(l, 1, None)
                pool.wait_ge(zeros_out, 16)
                wait_all_evacuated(pool, G_AT[f"tok{l}"] + 6)
                pool.wait_ge(idx_ready, l + 1)
                for k in range(2):
                    for t in range(TT):
                        nc.gpsimd.indirect_dma_start(
                            out=slots[:, :], out_offset=bass.IndirectOffsetOnAxis(ap=idx[:, k, t:t + 1], axis=0),
                            in_=tok[:, t, :], in_offset=None).then_inc(S["slots_filled"], 16)
                pool.wait_ge(S["slots_filled"], 96)
                pool.dma_start(xraw[:], slots[0:SLOT_TOK, :]).then_inc(S["xraw0_in"], 16)
                pool.wait_ge(all_stored, l + 1)
                for t in range(TT):
                    for k in range(2):
                        nc.gpsimd.indirect_dma_start(
                            out=gath[:, k, t, :], out_offset=None, in_=slots[:, :],
                            in_offset=bass.IndirectOffsetOnAxis(ap=idx[:, k, t:t + 1], axis=0)).then_inc(S[f"rows_back{t}_"], 16)

            pool.wait_ge(Y_ready, 6)
            load_rows(0, 0, A["hy_b_out"])
            moe_side(0)
            pool.wait_ge(ln_done, TT * 2)
            for i in range(2):
                src = A["na_rpb_rev"]
                first = RPB_H - (WIN_ROWS - 3) * RPB_C - WIN_COLS - (RPB_WIN - 1) + i * RPB_C
                pool.dma_start(rpb[i * GRID_W:(i + 1) * GRID_W, :, :],
                               bass.AP(src.tensor, first, [[1, GRID_W], [RPB_H, HEADS], [1, RPB_WIN]])).then_inc(att_in, 16)
            pool.dma_start(kraw[:].rearrange("t (h d) -> t h d", d=DH),
                           A["cache_k"][0, 0].rearrange("h t d -> t h d")).then_inc(att_in, 16)
            pool.dma_start(vctx[:].rearrange("t (h d) -> t h d", d=DH),
                           A["cache_v"][0, 0].rearrange("h t d -> t h d")).then_inc(att_in, 16)
            row_to_all(bv[:], A["na_b_qkv"][:, 2 * D:3 * D], D).then_inc(att_in, 16)
            pool.wait_ge(att_in, 80)
            pool.wait_ge(dft_in, 48)
            for n in range(2 * HEADS):
                if n >= 4:
                    pool.wait_ge(max_ready, HEADS + n - 3)
                e0 = (2 - 2 * (n // HEADS)) * RPB_C
                win = rpb[:, n % HEADS, RPB_WIN - 1 - e0:RPB_WIN - e0]
                nc.gpsimd.tensor_tensor(
                    bm[:, n % 4, :].rearrange("p (r c) -> p r c", c=GRID_W),
                    bass.AP(win.tensor, win.offset, [list(win.ap[0]), [-RPB_C, ROWS], [-1, GRID_W]]),
                    band[:].unsqueeze(1).to_broadcast([128, ROWS, GRID_W]), ALU.add).then_inc(bm_ready, 1)
            pool.wait_ge(o_evac, 6)
            pool.wait_ge(kv_out, 32)
            load_rows(1, 0, A["na_b_out"])
            moe_side(1)

        @block.tensor
        def _(pe):
            def bank(g):
                if g >= 8:
                    wait_evacuated(pe, g - 8)
                return ps[g % 8]

            def mm(out, lhsT, rhs, first=True, last=True):
                return nc.tensor.matmul(out, lhsT, rhs, start=first, stop=last)

            def ada(l, seg):
                name, first, count = ADA_SEG[l][seg]
                for n in range(count + 1):
                    if n < count:
                        i = ada_piece(l, first + n)
                        out = bank(G_AT[name] + ada_row(n))
                        wait_weights(pe, i)
                        w = w_view(i, 8, 512)
                        for k in range(KT):
                            last = mm(out[0:2, :], scond[:, k, :], w[:, k, :], k == 0, k == KT - 1)
                        last.then_inc(group_ready, 1)
                    if n >= 1:
                        out = bank(G_AT[name] + ada_col(n - 1, count))
                        wait_evacuated(pe, G_AT[name] + ada_row(n - 1))
                        for f in range(4):
                            last = nc.tensor.transpose(out[:, 2 * f:2 * f + 2],
                                                       arow(l, seg)[:, (first + n - 1) % 2, f * 128:(f + 1) * 128],
                                                       ident[0:2, 0:2])
                        last.then_inc(group_ready, 1)

            def gates(name, l, first_col):
                for c in range(2):
                    for h in range(2):
                        g = G_AT[name] + 2 * c + h
                        out = bank(g)
                        for j in range(4):
                            col = mod[l][:, first_col + 4 * h + j, c:c + 1]
                            last = mm(out[:, j * 128:(j + 1) * 128], col.to_broadcast([128, 128]), ident[:])
                        last.then_inc(group_ready, 1)

            def transpose_tiles(name, src, count):
                for j in range(count):
                    out = bank(G_AT[name] + j)
                    for t in range(TT):
                        last = nc.tensor.transpose(out[:, t * 128:(t + 1) * 128], src[:, t, j * 128:(j + 1) * 128], ident[:])
                    last.then_inc(group_ready, 1)

            def to_tokens(name, src):
                for t in range(TT):
                    for h in range(2):
                        out = bank(G_AT[name] + 2 * t + h)
                        for j in range(4):
                            last = nc.tensor.transpose(out[:, j * 128:(j + 1) * 128], src(4 * h + j, t), ident[:])
                        last.then_inc(group_ready, 1)

            pe.wait_ge(first_in, 128)
            out = bank(0)
            nc.tensor.transpose(out[:, 0:128], V1[:], ident[:]).then_inc(group_ready, 1)
            out = bank(1)
            nc.tensor.transpose(out[:, 0:120], V2[0:120, :], ident[0:120, 0:120]).then_inc(group_ready, 1)
            pe.wait_ge(scond_ready, 1)
            ada(0, 0)

            pe.wait_ge(filt_in, 144)
            mm(bank(G_AT["mlp0"])[0:FH, 0:TOK], fw1[:], feat[:]).then_inc(group_ready, 1)
            ada(0, 1)
            pe.wait_ge(mh_ready, 1)
            mm(bank(G_AT["mlp1"])[0:FH, 0:TOK], fw2[:], mh1[:]).then_inc(group_ready, 1)
            ada(0, 2)
            pe.wait_ge(mh_ready, 2)
            for t in range(TT):
                for h in range(2):
                    for d in range(2):
                        mm(bank(G_AT["filt"] + 4 * t + 2 * h + d)[:, :], mh2[:, t * 128:(t + 1) * 128],
                           fw3[:, d * D + h * 512:d * D + (h + 1) * 512]).then_inc(group_ready, 1)
            ada(0, 3)

            Cs = dft[:, 0:512].rearrange("p (k f) -> p k f", k=2)
            Ss = dft[:, 512:1024].rearrange("p (k f) -> p k f", k=2)
            Ci = dft[:, 1024:1536].rearrange("p (k f) -> p k f", k=2)
            Si = dft[:, 1536:2048].rearrange("p (k f) -> p k f", k=2)
            Cp, Sp, Cpi, Spi = (dft[:, 2048 + 128 * q:2176 + 128 * q] for q in range(4))

            def spectrum(name, cos_src, sin_src):
                for q in range(3):
                    for h in range(2):
                        for r in range(2):
                            out = bank(G_AT[name] + 4 * q + 2 * h + r)
                            src = (cos_src, sin_src)[r]
                            cs = slice(h * 512, (h + 1) * 512)
                            if q == 0:
                                last = mm(out[:, :], (Cp, Sp)[r], src[:, 0, cs])
                            else:
                                for k in range(2):
                                    last = mm(out[:, :], (Cs, Ss)[r][:, k, (q - 1) * 128:q * 128], src[:, 1 + k, cs],
                                              k == 0, k == 1)
                            last.then_inc(group_ready, 1)

            pe.wait_ge(dft_in, 48)
            pe.wait_ge(taps_ready, 1)
            spectrum("filtK", hsum, hdif)

            pe.wait_ge(mod_ready, 1)
            gates("gm0", 0, 16)
            pe.wait_ge(x_in, 32)
            transpose_tiles("xm0", x, KT)
            wait_all_evacuated(pe, G_AT["in"])
            for s in range(IN_W):
                i = W_AT["in"] + s
                wait_weights(pe, i)
                w = w_view(i, 8, 512)
                for f in range(4):
                    out = bank(G_AT["in"] + 4 * s + f)
                    for k in range(KT):
                        last = mm(out[:, 0:TOK], w[:, k, f * 128:(f + 1) * 128], hT[:, k, :], k == 0, k == KT - 1)
                    last.then_inc(group_ready, 1)
            pe.wait_ge(u_ready, 1)
            to_tokens("ut", lambda j, t: uT[:, j, TILE_AT[t]:TILE_AT[t] + 128])
            wait_all_evacuated(pe, G_AT["dft"])
            spectrum("dft", tok, tok)
            pe.wait_ge(Y_ready, 6)
            for j in range(KT):
                out = bank(G_AT["inv"] + j)
                js = slice(j * 128, (j + 1) * 128)
                mm(out[:, 0:128], Y[:, 0, 0, js], Cpi, True, False)
                mm(out[:, 0:128], Y[:, 0, 1, js], Spi, False, True)
                n = 0
                for q in range(2):
                    for r in range(2):
                        last = mm(out[:, 128:TOK], Y[:, 1 + q, r, js], (Ci, Si)[r][:, q, :], n == 0, n == 3)
                        n += 1
                last.then_inc(group_ready, 1)
            wait_all_evacuated(pe, G_AT["out0"])

            def project_out(l, src):
                for t in range(TT):
                    for h in range(OUT_W):
                        i = W_AT[f"out{l}"] + h
                        wait_weights(pe, i)
                        w = w_view(i, 8, 512)
                        out = bank(G_AT[f"out{l}"] + OUT_W * t + h)
                        for k in range(KT):
                            last = mm(out[:, :], src[:, k, t * 128:(t + 1) * 128], w[:, k, :], k == 0, k == KT - 1)
                        last.then_inc(group_ready, 1)

            def moe(l):
                S = moe_sems[l]
                if l == 0:
                    ada(1, 0)
                gates(f"gf{l}", l, 40)
                pe.wait_ge(ln_done, TT * (2 * l + 1))
                transpose_tiles(f"xf{l}", x, KT)
                wait_all_evacuated(pe, G_AT[f"logit{l}"])
                pe.wait_ge(moe_in, 80 * (l + 1))
                out = bank(G_AT[f"logit{l}"])
                for t in range(TT):
                    for k in range(KT):
                        last = mm(out[:, 20 * t:20 * t + 20], hT[:, k, t * 128:(t + 1) * 128], wr[:, k, :], k == 0, k == KT - 1)
                last.then_inc(group_ready, 1)
                if l == 0:
                    ada(1, 1)
                pe.wait_ge(M_ready, l + 1)
                out = bank(G_AT[f"rank{l}"])
                tri, ones = mc[:, MC_TRI:MC_TRI + 128], mc[:, MC_ONES:MC_ONES + 128]
                for t in range(TT):
                    for u in range(t):
                        mm(out[:, 16 * t:16 * t + 16], ones, Msel[:, u, :], u == 0, False)
                    mm(out[:, 16 * t:16 * t + 16], tri, Msel[:, t, :], t == 0, True)
                for u in range(TT):
                    last = mm(out[:, 48:64], ones, Msel[:, u, :], u == 0, u == TT - 1)
                last.then_inc(group_ready, 1)
                to_tokens(f"tok{l}", lambda j, t: hT[:, j, t * 128:(t + 1) * 128])
                if l == 0:
                    ada(1, 2)
                wait_all_evacuated(pe, G_AT["ada1c"] + 4 if l == 0 else G_AT["tok1"] + 6)
                pe.wait_ge(nb_ready, l + 1)
                first = W_AT[f"moe{l}"]

                def flip_block():
                    for k in range(KT):
                        last = nc.tensor.transpose(ps[(0, 5)[k // 4]][:, (k % 4) * 128:(k % 4 + 1) * 128],
                                                   xraw[:, k * 128:(k + 1) * 128], ident[:])
                    last.then_inc(S["flip_ready"], 1)

                pe.wait_ge(S["xraw0_in"], 16)
                flip_block()
                with pe.Fori(0, EXPERTS // 2) as p:
                    for half in range(2):
                        i0 = first + 3 * half
                        nb = pe.value_load(NBi[0:1, bass.ds(2 * p + half, 1)], min_val=1, max_val=MAX_NB)
                        base = pe.value_load(NBi[0:1, bass.ds(2 * p + half + 16, 1)], min_val=0, max_val=MAX_BLOCKS)
                        for c in range(3):
                            pe.wait_ge(w_loaded[(i0 + c) % RING], 16 * p + 16 * ((i0 + c) // RING + 1))
                            mm(ps[7][0:2, 0:2], ident[:, 0:2], ident[:, 0:2])
                        wa, wb, wd = w_view(i0, 8, 512), w_view(i0 + 1, 8, 512), w_view(i0 + 2, 4, 1024)
                        with pe.Fori(0, nb) as b:
                            w1 = base + b + 1
                            pe.wait_ge(S["xg_ready"], w1 * 2)
                            for out, w, name in ((ps[1], wa, "a_ready"), (ps[2], wb, "b_ready")):
                                for f in range(4):
                                    for k in range(KT):
                                        last = mm(out[:, f * SLOT_TOK:(f + 1) * SLOT_TOK], w[:, k, f * 128:(f + 1) * 128],
                                                  xg[:, k, :], k == 0, k == KT - 1)
                                last.then_inc(S[name], 1)
                            pe.wait_ge(S["xraw_in"], w1 * 16)
                            flip_block()
                            pe.wait_ge(S["he_ready"], w1)
                            for h in range(2):
                                for k in range(4):
                                    last = mm(ps[3 + h][0:SLOT_TOK, :], he[:, k, :], wd[:, k, h * 512:(h + 1) * 512],
                                              k == 0, k == 3)
                                last.then_inc(S[f"y{h}_ready"], 1)
                        mm(ps[7][0:2, 0:2], ident[:, 0:2], ident[:, 0:2]).then_inc(expert_done[l], 1)
                pe.wait_ge(blocks_done, 2 * l + 2)

            project_out(0, yT)
            moe(0)

            ada(1, 3)
            pe.wait_ge(mod_ready, 2)
            gates("gm1", 1, 16)
            pe.wait_ge(ln_done, TT * 2)
            transpose_tiles("xm1", x, KT)
            wait_all_evacuated(pe, G_AT["qk"])
            for s in range(4):
                i = W_AT["qkv"] + s
                wait_weights(pe, i)
                w = w_view(i, 8, 512)
                for f in range(4):
                    out = bank(G_AT["qk"] + 4 * s + f)
                    for k in range(KT):
                        last = mm(out[:, 0:TOK], w[:, k, f * 128:(f + 1) * 128], hT[:, k, :], k == 0, k == KT - 1)
                    last.then_inc(group_ready, 1)
            for h in range(2):
                i = W_AT["qkv"] + 4 + h
                wait_weights(pe, i)
                w = w_view(i, 8, 512)
                for t in range(TT):
                    out = bank(G_AT["v"] + TT * h + t)
                    for k in range(KT):
                        last = mm(out[:, :], hT[:, k, t * 128:(t + 1) * 128], w[:, k, :], k == 0, k == KT - 1)
                    last.then_inc(group_ready, 1)
            pe.wait_ge(att_in, 80)
            for h in range(2):
                out = bank(G_AT["kout"] + h)
                for j in range(4):
                    last = nc.tensor.transpose(out[:, j * 128:(j + 1) * 128], kraw[:, (4 * h + j) * 128:(4 * h + j + 1) * 128], ident[:])
                last.then_inc(group_ready, 1)
            for h in range(2):
                out = bank(G_AT["kctx"] + h)
                for j in range(4):
                    last = nc.tensor.transpose(out[:, j * 128:(j + 1) * 128], kT[:, 4 * h + j, 0:128], ident[:])
                last.then_inc(group_ready, 1)
            wait_all_evacuated(pe, G_AT["ot"])

            units = TT * HEADS

            def scores(u):
                t, h = divmod(u, HEADS)
                lo = DH * (h % 2)
                if u >= 3:
                    pe.wait_ge(p_ready, u - 2)
                q = qT[lo:lo + DH, h // 2, t * 128:(t + 1) * 128]
                if t == 0:
                    last = mm(ps[u % 3][:, 0:128], q, kT[lo:lo + DH, h // 2, 0:PROMPT])
                else:
                    mm(ps[u % 3][:, 0:256], q, kT[lo:lo + DH, h // 2, PROMPT:TOK])
                    last = mm(ps[u % 3][:, 256:384], q, kctxT[lo:lo + DH, h // 2, :])
                last.then_inc(s_ready, 1)

            def flip(u):
                pe.wait_ge(p_ready, u + 1)
                if u >= 2:
                    pe.wait_ge(pt_ready, u - 1)
                for c in range(1 if u < HEADS else 3):
                    last = nc.tensor.transpose(ps[3 + u % 2][:, c * 128:(c + 1) * 128], P[:, u % 3, c * 128:(c + 1) * 128], ident[:])
                last.then_inc(t_ready, 1)

            def weigh(u):
                t, h = divmod(u, HEADS)
                half = u // 8
                if u % 8 == 0 and half >= 3:
                    pe.wait_ge(o_evac, half - 2)
                pe.wait_ge(pt_ready, u + 1)
                out = ps[5 + half % 3][:, (h % 8) * DH:(h % 8 + 1) * DH]
                hs = slice(h * DH, (h + 1) * DH)
                if t == 0:
                    last = mm(out, PT[:, u % 2, 0:128], tok[:, 0, hs])
                else:
                    mm(out, PT[:, u % 2, 0:128], tok[:, 1, hs], True, False)
                    mm(out, PT[:, u % 2, 128:256], tok[:, 2, hs], False, False)
                    last = mm(out, PT[:, u % 2, 256:384], vctx[:, hs], False, True)
                last.then_inc(pv_done, 1)

            for n in range(units + 3):
                if n < units:
                    scores(n)
                if 0 <= n - 2 < units:
                    flip(n - 2)
                if 0 <= n - 3 < units:
                    weigh(n - 3)
            pe.wait_ge(o_evac, 6)
            transpose_tiles("ot", otok, KT)
            wait_all_evacuated(pe, G_AT["out1"])
            project_out(1, oT)
            moe(1)

        @block.scalar
        def _(act):
            act.dma_start(V1[0:96, :], A["b_ada"].rearrange("l (f p) -> (l f) p", p=128)).then_inc(first_in, 16)
            act.dma_start(V1[96:104, :], A["c_ctx"].rearrange("(f p) -> f p", p=128)).then_inc(first_in, 16)
            act.dma_start(V1[104:112, :], A["c"].rearrange("a (f p) -> (a f) p", p=128)).then_inc(first_in, 16)
            act.dma_start(V1[112:128, :], A["na_b_qkv"][:, 0:2 * D].rearrange("a (f p) -> (a f) p", p=128)).then_inc(first_in, 16)
            act.dma_start(ident[:], A["k_ident"]).then_inc(first_in, 16)
            act.dma_start(V2[0:24, :], A["hy_b_in"].rearrange("a (f p) -> (a f) p", p=128)).then_inc(first_in, 16)
            act.dma_start(V2[24:96, :], A["hy_conv_w"][0].rearrange("j (f p) -> (j f) p", p=128)).then_inc(first_in, 16)
            act.dma_start(V2[96:120, :], A["hy_conv_b"].rearrange("a (f p) -> (a f) p", p=128)).then_inc(first_in, 16)
            act.dma_start(x[:, 0, :], A["x_prompt"][0]).then_inc(x_in, 16)
            act.dma_start(x[:, 1:3, :], A["x_sample"][0].rearrange("(t p) d -> p t d", p=128)).then_inc(x_in, 16)

            act.wait_ge(cond_cols, 1)
            nc.scalar.activation(scond[:, :, :].rearrange("p k c -> p c k"),
                                 VT[:, V_CC:V_CC + 16].rearrange("p (c k) -> p c k", c=2), ACT.Silu).then_inc(scond_ready, 1)

            def ada(l, seg, from_=0, to=ADA_W + 1):
                name, first, count = ADA_SEG[l][seg]
                for n in range(from_, min(to, count + 1)):
                    if n < count:
                        g = G_AT[name] + ada_row(n)
                        wait_group(act, g)
                        nc.scalar.activation(arow(l, seg)[:, (first + n) % 2, :], ps[g % 8][0:2, :], ACT.Copy
                                             ).then_inc(evacuated[g % 8], 1)
                    if n >= 1:
                        g = G_AT[name] + ada_col(n - 1, count)
                        f = 4 * (first + n - 1)
                        wait_group(act, g)
                        nc.scalar.activation(mod[l][:, f:f + 4, :].rearrange("p f c -> p (f c)"), ps[g % 8][:, 0:8],
                                             ACT.Copy).then_inc(evacuated[g % 8], 1)

            ada(0, 0)
            act.wait_ge(marg_ready, 1)
            nc.scalar.activation(mh1[:], marg[:], ACT.Sin).then_inc(mh_ready, 1)
            act.wait_ge(dabs_ready, 1)
            for t in range(TT):
                nc.scalar.activation(decay[:, t, :], dabs[:], ACT.Exp, scale=cols[:, t:t + 1]).then_inc(decay_ready, 1)
                ada(0, 1, t, t + 1)
            act.wait_ge(marg_ready, 2)
            nc.scalar.activation(mh2[:], marg[:], ACT.Sin).then_inc(mh_ready, 1)
            ada(0, 2)
            ada(0, 3)
            act.wait_ge(taps_ready, 1)
            for n in range(12):
                g = G_AT["filtK"] + n
                q, h, r = n // 4, n // 2 % 2, n % 2
                wait_group(act, g)
                nc.scalar.activation(K[:, q, r, h * 512:(h + 1) * 512], ps[g % 8][:, :], ACT.Copy).then_inc(evacuated[g % 8], 1)

            def modulate_odd(name, l, shift, scale):
                for j in range(1, KT, 2):
                    g = G_AT[name] + j
                    wait_group(act, g)
                    for c, (a, b) in enumerate(((0, PROMPT), (PROMPT, TOK))):
                        last = nc.scalar.activation(hT[:, j, a:b], ps[g % 8][:, a:b], ACT.Identity,
                                                    bias=mod[l][:, shift + j, c:c + 1], scale=mod[l][:, scale + j, c:c + 1])
                    last.then_inc(evacuated[g % 8], 1)

            act.wait_ge(mod_ready, 1)
            modulate_odd("xm0", 0, 0, 8)

            act.wait_ge(guards_ready, 1)
            for n in range(24):
                g = G_AT["in"] + n
                wait_group(act, g)
                if n >= 2:
                    act.wait_ge(z_used, n - 1)
                for a, b, at_ in SEQ_AT:
                    last = nc.scalar.activation(zt[:, n % 2, at_:at_ + b - a], ps[g % 8][:, a:b], ACT.Identity,
                                                bias=VT[:, V_BIN + n:V_BIN + n + 1])
                last.then_inc(evacuated[g % 8], 1)
            act.wait_ge(z_used, 24)
            act.wait_ge(u_ready, 1)
            for n in range(6):
                g = G_AT["ut"] + n
                wait_group(act, g)
                nc.scalar.activation(tok[:, n // 2, (n % 2) * 512:(n % 2 + 1) * 512], ps[g % 8][:, :], ACT.Copy
                                     ).then_inc(evacuated[g % 8], 1)

            def normalize(n, t):
                act.wait_ge(var_ready, TT * n + t + 1)
                nc.scalar.activation(sd[:, 0, t:t + 1], sd[:, 1, t:t + 1], ACT.Sqrt).then_inc(sd_ready, 1)
                act.wait_ge(mean_ready, TT * n + t + 1)
                nc.scalar.activation(x[:, t, :], x[:, t, :], ACT.Identity, bias=sd[:, 2, t:t + 1], scale=sd[:, 0, t:t + 1]
                                     ).then_inc(norm_done, 1)

            def moe(l):
                S = moe_sems[l]
                for t in range(TT):
                    normalize(2 * l, t)
                if l == 0:
                    ada(1, 0)
                modulate_odd(f"xf{l}", l, 24, 32)
                if l == 0:
                    ada(1, 1)
                act.wait_ge(ex_ready, l + 1)
                nc.scalar.activation(ex[:], ex[:], ACT.Exp).then_inc(ex_done, 1)
                for n in range(6):
                    g = G_AT[f"tok{l}"] + n
                    wait_group(act, g)
                    nc.scalar.activation(tok[:, n // 2, (n % 2) * 512:(n % 2 + 1) * 512], ps[g % 8][:, :], ACT.Copy
                                         ).then_inc(evacuated[g % 8], 1)
                if l == 0:
                    ada(1, 2)
                act.wait_ge(S["flip_ready"], 1)
                nc.scalar.activation(xg[:, 4:8, :].rearrange("p k s -> p (k s)"), ps[5][:, :], ACT.Copy).then_inc(S["xg_ready"], 1)
                act.dma_start(xraw[:], slots[SLOT_TOK:2 * SLOT_TOK, :]).then_inc(S["xraw_in"], 16)
                act.wait_ge(nb_ready, l + 1)
                total = act.value_load(NBi[0:1, 32:33], min_val=EXPERTS, max_val=MAX_BLOCKS)
                with act.Fori(0, total) as b:
                    act.wait_ge(S["a_ready"], b + 1)
                    nc.scalar.activation(sa[:].rearrange("p f s -> p (f s)"), ps[1][:, 0:4 * SLOT_TOK], ACT.Silu
                                         ).then_inc(S["sa_ready"], 1)
                    act.wait_ge(S["flip_ready"], b + 2)
                    nc.scalar.activation(xg[:, 4:8, :].rearrange("p k s -> p (k s)"), ps[5][:, :], ACT.Copy).then_inc(S["xg_ready"], 1)
                    act.dma_start(xraw[:], slots[bass.ds(b * SLOT_TOK + 2 * SLOT_TOK, SLOT_TOK), :]).then_inc(S["xraw_in"], 16)
                    act.wait_ge(S["y1_ready"], b + 1)
                    act.wait_ge(S["y_stored"], b * 16 + 16)
                    nc.scalar.activation(ysb[:, 512:1024], ps[4][0:SLOT_TOK, :], ACT.Copy).then_inc(S["ysb1_ready"], 1)
                    act.wait_ge(S["ysb0_ready"], b + 1)
                    act.wait_ge(S["ysb1_ready"], b + 1)
                    act.dma_start(slots[bass.ds(b * SLOT_TOK, SLOT_TOK), :], ysb[:]).then_inc(S["y_stored"], 16)
                nc.scalar.activation(credit[:, 3:4], ident[:, 0:1], ACT.Copy).then_inc(blocks_done, 1)
                act.wait_ge(S["y_stored"], total * 16 + 16)
                act.wait_ge(S["xraw_in"], total * 16 + 16)
                nc.scalar.activation(credit[:, 1:2], ident[:, 0:1], ACT.Copy).then_inc(all_stored, 1)

                def scale_first(t):
                    act.wait_ge(S[f"rows_back{t}_"], 32)
                    nc.scalar.activation(gath[:, 0, t, :], gath[:, 0, t, :], ACT.Copy, scale=wk[:, 0, t:t + 1]
                                         ).then_inc(first_scaled, 1)

                if l == 0:
                    act.wait_ge(blocks_done, 2)
                    ada(1, 3, 0, 1)
                scale_first(0)
                scale_first(1)
                if l == 0:
                    ada(1, 3, 1, 2)
                normalize(2 * l + 1, 0)
                scale_first(2)
                if l == 0:
                    ada(1, 3, 2, 3)
                normalize(2 * l + 1, 1)
                normalize(2 * l + 1, 2)
                if l == 0:
                    ada(1, 3, 3)

            moe(0)

            act.wait_ge(mod_ready, 2)
            modulate_odd("xm1", 1, 0, 8)
            for j in range(KT):
                g = G_AT["qk"] + KT + j
                wait_group(act, g)
                nc.scalar.activation(kT[:, j, :], ps[g % 8][:, 0:TOK], ACT.Identity,
                                     bias=VT[:, V_BQK + KT + j:V_BQK + KT + j + 1]).then_inc(evacuated[g % 8], 1)
            for g in (G_AT["v"], G_AT["v"] + TT):
                wait_evacuated(act, g)
            act.dma_start(new_v[0, 0].rearrange("h t d -> t h d"), tok[:, 0, :].rearrange("t (h d) -> t h d", d=DH)
                          ).then_inc(kv_out, 16)
            for h in range(2):
                g = G_AT["kout"] + h
                wait_group(act, g)
                nc.scalar.activation(kctxT[:, 4 * h:4 * h + 4, :].rearrange("p j t -> p (j t)"), ps[g % 8][:, :], ACT.Copy
                                     ).then_inc(evacuated[g % 8], 1)
            for h in range(2):
                g = G_AT["kctx"] + h
                wait_group(act, g)
                nc.scalar.activation(kst[:, h * 512:(h + 1) * 512], ps[g % 8][:, :], ACT.Copy).then_inc(evacuated[g % 8], 1)
            for h in range(2):
                wait_evacuated(act, G_AT["kctx"] + h)
            act.dma_start(new_k[0, 0].rearrange("h t d -> t h d"), kst[:].rearrange("t (h d) -> t h d", d=DH)
                          ).then_inc(kv_out, 16)

            units = TT * HEADS

            def exponentials(u):
                n = 128 if u < HEADS else 384
                act.wait_ge(max_ready, u + 1)
                if u >= 3:
                    act.wait_ge(t_ready, u - 2)
                nc.scalar.activation(P[:, u % 3, 0:n], ps[u % 3][:, 0:n], ACT.Exp, bias=nmax[:, u:u + 1],
                                     accum_out=den[:, u:u + 1]).then_inc(p_ready, 1)

            def flipped(u):
                n = 128 if u < HEADS else 384
                act.wait_ge(t_ready, u + 1)
                if u >= 2:
                    act.wait_ge(pv_done, u - 1)
                nc.scalar.activation(PT[:, u % 2, 0:n], ps[3 + u % 2][:, 0:n], ACT.Copy).then_inc(pt_ready, 1)

            for n in range(units + 2):
                if n < units:
                    exponentials(n)
                if n >= 2:
                    flipped(n - 2)
            moe(1)
            act.wait_ge(kv_out, 32)

        @block.vector
        def _(dve):
            v = nc.vector
            steps = [0]

            def link(ins):
                steps[0] += 1
                ins.then_inc(dve_step, 1)
                dve.wait_ge(dve_step, steps[0])

            for g, n in ((0, 128), (1, 120)):
                wait_group(dve, g)
                last = v.tensor_copy(VT[:, 128 * g:128 * g + n], ps[g][:, 0:n])
                last.then_inc(evacuated[g], 1)
                if g == 0:
                    wait_evacuated(dve, 0)
                    v.memset(credit[:, 4:5], 0.0).then_inc(cond_cols, 1)
            wait_evacuated(dve, 1)

            def ada(l):
                name, _, count = ADA_SEG[l][-1]
                wait_all_evacuated(dve, G_AT[name] + 2 * count)
                link(v.tensor_tensor(mod[l][:], mod[l][:], VT[:, V_ADA + 48 * l:V_ADA + 48 * l + 48].unsqueeze(2
                                     ).to_broadcast([128, 48, 2]), ALU.add))
                link(v.tensor_scalar_add(mod[l][:, 8:16, :], mod[l][:, 8:16, :], 1.0))
                v.tensor_scalar_add(mod[l][:, 32:40, :], mod[l][:, 32:40, :], 1.0).then_inc(mod_ready, 1)
                dve.wait_ge(mod_ready, l + 1)

            dve.wait_ge(filt_in, 144)
            v.scalar_tensor_tensor(out=dabs[:], in0=dabs[:], scalar=-1.0, in1=dabs[:], op0=ALU.mult, op1=ALU.max).then_inc(dabs_ready, 1)
            two_pi = 2.0 * math.pi
            c1 = float(np.float32(6.28125))
            c2 = float(np.round((two_pi - c1) * 2 ** 20) / 2 ** 20)
            c3 = float(np.float32(two_pi - c1 - c2))
            magic = float(1.5 * 2 ** 23)
            for n in range(2):
                g = G_AT[f"mlp{n}"]
                wait_group(dve, g)
                v.tensor_scalar(marg[:], ps[g % 8][0:FH, 0:TOK], fcol[:, n:n + 1], fcol[:, 2:3], ALU.add, ALU.mult
                                ).then_inc(evacuated[g % 8], 1)
                wait_evacuated(dve, g)
                link(v.tensor_scalar(mrnd[:], marg[:], 1.0 / two_pi, magic, ALU.mult, ALU.add))
                link(v.tensor_scalar_add(mrnd[:], mrnd[:], -magic))
                for c in (c1, c2, c3):
                    link(v.scalar_tensor_tensor(out=marg[:], in0=mrnd[:], scalar=-c, in1=marg[:], op0=ALU.mult, op1=ALU.add))
                v.tensor_scalar(marg[:], marg[:], 3.1415925, -3.1415925, ALU.min, ALU.max).then_inc(marg_ready, 1)

            for t in range(TT):
                dve.wait_ge(decay_ready, t + 1)
                for h in range(2):
                    hs = slice(h * 512, (h + 1) * 512)
                    g = G_AT["filt"] + 4 * t + 2 * h
                    for d in range(2):
                        wait_group(dve, g + d)
                        v.tensor_tensor(ftmp[:, d, :], ps[(g + d) % 8][:, :],
                                        decay[:, t, d * D + h * 512:d * D + (h + 1) * 512], ALU.mult
                                        ).then_inc(evacuated[(g + d) % 8], 1)
                    wait_evacuated(dve, g)
                    wait_evacuated(dve, g + 1)
                    link(v.scalar_tensor_tensor(out=hsum[:, t, hs], in0=ftmp[:, 1, :], scalar=cols[:, 3 + t:4 + t],
                                                in1=ftmp[:, 0, :], op0=ALU.mult, op1=ALU.add))
                    link(v.tensor_tensor(hdif[:, t, hs], ftmp[:, 0, :], ftmp[:, 1, :], ALU.subtract))
            dve.wait_ge(dft_in, 48)
            skip = tmp[0:1, :, :].rearrange("p a n -> p (a n)")
            link(v.tensor_tensor(hsum[0:1, 0, :], hsum[0:1, 0, :], skip, ALU.add))
            v.tensor_tensor(hsum[0:1, 1, :], hsum[0:1, 1, :], skip, ALU.add).then_inc(taps_ready, 1)
            dve.wait_ge(taps_ready, 1)
            ada(0)

            def gates(name):
                for n in range(4):
                    g = G_AT[name] + n
                    wait_group(dve, g)
                    v.tensor_copy(gate[:, n // 2, (n % 2) * 512:(n % 2 + 1) * 512], ps[g % 8][:, :]).then_inc(evacuated[g % 8], 1)

            def modulate_even(name, l, shift, scale):
                for j in range(0, KT, 2):
                    g = G_AT[name] + j
                    wait_group(dve, g)
                    for c, (a, b) in enumerate(((0, PROMPT), (PROMPT, TOK))):
                        last = v.tensor_scalar(hT[:, j, a:b], ps[g % 8][:, a:b], mod[l][:, scale + j, c:c + 1],
                                               mod[l][:, shift + j, c:c + 1], ALU.mult, ALU.add)
                    last.then_inc(evacuated[g % 8], 1)

            gates("gm0")
            link(v.memset(zt[:], 0.0))
            v.memset(acc[:], 0.0).then_inc(guards_ready, 1)
            dve.wait_ge(guards_ready, 1)
            modulate_even("xm0", 0, 0, 8)

            for n in range(24):
                g = G_AT["in"] + n
                part, j = divmod(n, KT)
                wait_evacuated(dve, g)
                z, a = zt[:, n % 2, :], acc[:, n % 2, :]
                W = PAD - 2
                tap = [VT[:, V_CW + 24 * i + n:V_CW + 24 * i + n + 1] for i in range(3)]
                link(v.tensor_scalar(a[:, 1:1 + W], z[:, 1:1 + W], tap[1], VT[:, V_CB + n:V_CB + n + 1], ALU.mult, ALU.add))
                link(v.scalar_tensor_tensor(out=a[:, 1:1 + W], in0=z[:, 0:W], scalar=tap[0], in1=a[:, 1:1 + W],
                                            op0=ALU.mult, op1=ALU.add))
                dst = (x0T[:, j, 1:1 + W], uT[:, j, 1:1 + W], a[:, 1:1 + W])[part]
                v.scalar_tensor_tensor(out=dst, in0=z[:, 2:2 + W], scalar=tap[2], in1=a[:, 1:1 + W],
                                       op0=ALU.mult, op1=ALU.add).then_inc(z_used, 1)
                dve.wait_ge(z_used, n + 1)
                if part == 2:
                    ins = v.tensor_tensor(uT[:, j, 1:1 + W], uT[:, j, 1:1 + W], a[:, 1:1 + W], ALU.mult)
                    if j == KT - 1:
                        ins.then_inc(u_ready, 1)
                    else:
                        link(ins)
            dve.wait_ge(zeros_out, 16)
            for n in range(6):
                q, h = divmod(n, 2)
                hs = slice(h * 512, (h + 1) * 512)
                gc = G_AT["dft"] + 2 * n
                wait_group(dve, gc)
                wait_group(dve, gc + 1)
                uc, us = ps[gc % 8], ps[(gc + 1) % 8]
                link(v.tensor_tensor(Y[:, q, 0, hs], uc[:, :], K[:, q, 0, hs], ALU.mult))
                v.tensor_tensor(Y[:, q, 1, hs], uc[:, :], K[:, q, 1, hs], ALU.mult).then_inc(evacuated[gc % 8], 1)
                link(v.tensor_tensor(tmp[:, 0, :], us[:, :], K[:, q, 1, hs], ALU.mult))
                v.tensor_tensor(tmp[:, 1, :], us[:, :], K[:, q, 0, hs], ALU.mult).then_inc(evacuated[(gc + 1) % 8], 1)
                wait_evacuated(dve, gc)
                wait_evacuated(dve, gc + 1)
                link(v.tensor_tensor(Y[:, q, 0, hs], Y[:, q, 0, hs], tmp[:, 0, :], ALU.subtract))
                v.tensor_tensor(Y[:, q, 1, hs], Y[:, q, 1, hs], tmp[:, 1, :], ALU.add).then_inc(Y_ready, 1)
                dve.wait_ge(Y_ready, n + 1)
            for j in range(KT):
                g = G_AT["inv"] + j
                wait_group(dve, g)
                for a, b, at_ in SEQ_AT:
                    last = v.tensor_tensor(yT[:, j, a:b], ps[g % 8][:, a:b], x0T[:, j, at_:at_ + b - a], ALU.mult)
                last.then_inc(evacuated[g % 8], 1)

            def statistics(t):
                for h in range(2):
                    link(v.bn_stats(st[:, t, h, :], x[:, t, h * 512:(h + 1) * 512]))
                link(v.bn_aggr(mv[:, t, :], st[:, t, :, :].rearrange("p a b -> p (a b)")))
                v.tensor_scalar_add(sd[:, 1, t:t + 1], mv[:, t, 1:2], LN_EPS).then_inc(var_ready, 1)

            def center(n, t):
                dve.wait_ge(sd_ready, TT * n + t + 1)
                link(v.reciprocal(sd[:, 0, t:t + 1], sd[:, 0, t:t + 1]))
                v.tensor_scalar(sd[:, 2, t:t + 1], mv[:, t, 0:1], sd[:, 0, t:t + 1], -1.0, ALU.mult, ALU.mult
                                ).then_inc(mean_ready, 1)

            def affine(n, t):
                dve.wait_ge(norm_done, TT * n + t + 1)
                link(v.tensor_tensor(x[:, t, :], x[:, t, :], rows[:, 1, :], ALU.mult))
                v.tensor_tensor(x[:, t, :], x[:, t, :], rows[:, 2, :], ALU.add).then_inc(ln_done, 1)

            def sum_and_norm(n, add_to_x):
                for t in range(TT):
                    add_to_x(t)
                    statistics(t)
                    if t > 0:
                        affine(n, t - 1)
                    center(n, t)
                affine(n, TT - 1)
                dve.wait_ge(ln_done, TT * (n + 1))

            def residual(l):
                dve.wait_ge(rows_in, 80 * l + 48)
                if l == 0:
                    dve.wait_ge(x_in, 32)

                def add_projection(t):
                    for h in range(OUT_W):
                        g = G_AT[f"out{l}"] + OUT_W * t + h
                        hs = slice(h * 512, (h + 1) * 512)
                        wait_group(dve, g)
                        buf = tmp[:, h, :]
                        v.tensor_tensor(buf, ps[g % 8][:, :], rows[:, 0, hs], ALU.add).then_inc(evacuated[g % 8], 1)
                        wait_evacuated(dve, g)
                        link(v.tensor_tensor(buf, buf, gate[:, COND[t], hs], ALU.mult))
                        link(v.scalar_tensor_tensor(out=x[:, t, hs], in0=x[:, t, hs], scalar=ALPHA, in1=buf,
                                                    op0=ALU.mult, op1=ALU.add))

                sum_and_norm(2 * l, add_projection)

            def first_of(dst, src, top):
                link(v.tensor_tensor(sc4[:], src, top.unsqueeze(2).to_broadcast([128, TT, 4]), ALU.is_equal))
                link(v.tensor_tensor(sc4[:], sc4[:], mc[:, MC_PREF:MC_PREF + 4].unsqueeze(1).to_broadcast([128, TT, 4]), ALU.mult))
                link(v.reduce_max(mx[:, 7, :], sc4[:], AX))
                link(v.tensor_tensor(dst, sc4[:], mx[:, 7, :].unsqueeze(2).to_broadcast([128, TT, 4]), ALU.is_equal))

            def moe(l):
                S = moe_sems[l]
                gates(f"gf{l}")
                modulate_even(f"xf{l}", l, 24, 32)
                g = G_AT[f"logit{l}"]
                wait_group(dve, g)
                dve.wait_ge(moe_in, 80 * (l + 1))
                v.tensor_tensor(Lg[:], ps[g % 8][:, 0:60].rearrange("p (t n) -> p t n", t=TT),
                                br[:].unsqueeze(1).to_broadcast([128, TT, 20]), ALU.add).then_inc(evacuated[g % 8], 1)
                wait_evacuated(dve, g)
                gl = Lg[:, :, 0:4]
                link(v.reduce_max(mx[:, 0, :], gl, AX))
                first_of(ohg[:], gl, mx[:, 0, :])
                pick = t256[:, 0:48].rearrange("p (t g j) -> p t g j", t=TT, g=4)
                link(v.tensor_tensor(pick, Lg[:, :, 4:20].rearrange("p t (g j) -> p t g j", g=4),
                                     ohg[:].unsqueeze(3).to_broadcast([128, TT, 4, 4]), ALU.mult))
                link(v.tensor_reduce(esel[:], pick.rearrange("p t g j -> p t j g"), AX, ALU.add))
                link(v.reduce_max(mx[:, 1, :], esel[:], AX))
                first_of(o1[:], esel[:], mx[:, 1, :])
                link(v.scalar_tensor_tensor(out=esel[:], in0=o1[:], scalar=NEG, in1=esel[:], op0=ALU.mult, op1=ALU.add))
                link(v.reduce_max(mx[:, 2, :], esel[:], AX))
                first_of(o2[:], esel[:], mx[:, 2, :])
                m4 = [m[:].rearrange("p t (g j) -> p t g j", g=4) for m in (M1, M2)]
                for m, oh in zip(m4, (o1, o2)):
                    link(v.tensor_tensor(m, ohg[:].unsqueeze(3).to_broadcast([128, TT, 4, 4]),
                                         oh[:].unsqueeze(2).to_broadcast([128, TT, 4, 4]), ALU.mult))
                v.tensor_tensor(Msel[:], M1[:], M2[:], ALU.add).then_inc(M_ready, 1)
                dve.wait_ge(M_ready, l + 1)
                link(v.tensor_tensor(ex[:, 0:12].rearrange("p (t g) -> p t g", t=TT), gl,
                                     mx[:, 0, :].unsqueeze(2).to_broadcast([128, TT, 4]), ALU.subtract))
                v.tensor_tensor(ex[:, 12:15], mx[:, 2, :], mx[:, 1, :], ALU.subtract).then_inc(ex_ready, 1)
                g = G_AT[f"rank{l}"]
                wait_group(dve, g)
                v.tensor_copy(R[:], ps[g % 8][:, 0:64]).then_inc(evacuated[g % 8], 1)
                wait_evacuated(dve, g)
                rk, cnt = R[:, 0:48].rearrange("p (t e) -> p t e", t=TT), R[:, 48:64]
                over = t256[:, 0:16 * MAX_NB].rearrange("p (e j) -> p e j", j=MAX_NB)
                link(v.tensor_tensor(over, cnt.unsqueeze(2).to_broadcast([128, 16, MAX_NB]),
                                     mc[:, MC_THR:MC_THR + MAX_NB].unsqueeze(1).to_broadcast([128, 16, MAX_NB]), ALU.is_gt))
                link(v.tensor_reduce(nbase[:, 0:16], over, AX, ALU.add))
                link(v.tensor_scalar_max(nbase[:, 0:16], nbase[:, 0:16], 1.0))
                before = t256[:, :].rearrange("p (e j) -> p e j", j=16)
                link(v.tensor_tensor(before, nbase[:, 0:16].unsqueeze(1).to_broadcast([128, 16, 16]),
                                     mc[:, MC_BEFORE:MC_BEFORE + 256].rearrange("p (e j) -> p e j", j=16), ALU.mult))
                link(v.tensor_reduce(nbase[:, 16:32], before, AX, ALU.add))
                link(v.tensor_tensor(nbase[:, 32:33], nbase[:, 15:16], nbase[:, 31:32], ALU.add))
                v.tensor_copy(NBi[:], nbase[:]).then_inc(nb_ready, 1)
                dve.wait_ge(nb_ready, l + 1)
                link(v.scalar_tensor_tensor(out=pos[:], in0=nbase[:, 16:32].unsqueeze(1).to_broadcast([128, TT, 16]),
                                            scalar=float(SLOT_TOK), in1=rk, op0=ALU.mult, op1=ALU.add))
                for k, m in enumerate((M1, M2)):
                    link(v.tensor_tensor(t48[:], m[:], pos[:], ALU.mult))
                    link(v.tensor_reduce(idxf[:, k, :], t48[:], AX, ALU.add))
                v.tensor_copy(idx[:], idxf[:]).then_inc(idx_ready, 1)
                dve.wait_ge(ex_done, l + 1)
                link(v.tensor_reduce(mx[:, 3, :], ex[:, 0:12].rearrange("p (t g) -> p t g", t=TT), AX, ALU.add))
                link(v.tensor_scalar_add(mx[:, 4, :], ex[:, 12:15], 1.0))
                link(v.tensor_tensor(mx[:, 3, :], mx[:, 3, :], mx[:, 4, :], ALU.mult))
                link(v.reciprocal(wk[:, 0, :], mx[:, 3, :]))
                link(v.tensor_tensor(wk[:, 1, :], wk[:, 0, :], ex[:, 12:15], ALU.mult))
                v.memset(credit[:, 2:3], 0.0).then_inc(S["y_stored"], 16)
                total = dve.value_load(NBi[0:1, 32:33], min_val=EXPERTS, max_val=MAX_BLOCKS)

                def flipped(n):
                    dve.wait_ge(S["flip_ready"], n)
                    v.tensor_copy(xg[:, 0:4, :].rearrange("p k s -> p (k s)"), ps[0][:, :]).then_inc(S["xg_ready"], 1)

                flipped(1)
                with dve.Fori(0, total) as b:
                    dve.wait_ge(S["b_ready"], b + 1)
                    dve.wait_ge(S["sa_ready"], b + 1)
                    v.tensor_tensor(he[:].rearrange("p f s -> p (f s)"), sa[:].rearrange("p f s -> p (f s)"),
                                    ps[2][:, 0:4 * SLOT_TOK], ALU.mult).then_inc(S["he_ready"], 1)
                    flipped(b + 2)
                    dve.wait_ge(S["y0_ready"], b + 1)
                    dve.wait_ge(S["y_stored"], b * 16 + 16)
                    v.tensor_copy(ysb[:, 0:512], ps[3][0:SLOT_TOK, :]).then_inc(S["ysb0_ready"], 1)
                v.memset(credit[:, 5:6], 0.0).then_inc(blocks_done, 1)
                dve.wait_ge(rows_in, 80 * (l + 1))

                def add_experts(t):
                    dve.wait_ge(first_scaled, TT * l + t + 1)
                    dve.wait_ge(S[f"rows_back{t}_"], 32)
                    link(v.scalar_tensor_tensor(out=gath[:, 0, t, :], in0=gath[:, 1, t, :], scalar=wk[:, 1, t:t + 1],
                                                in1=gath[:, 0, t, :], op0=ALU.mult, op1=ALU.add))
                    link(v.tensor_tensor(gath[:, 0, t, :], gath[:, 0, t, :], gate[:, COND[t], :], ALU.mult))
                    link(v.scalar_tensor_tensor(out=x[:, t, :], in0=x[:, t, :], scalar=ALPHA, in1=gath[:, 0, t, :],
                                                op0=ALU.mult, op1=ALU.add))

                sum_and_norm(2 * l + 1, add_experts)

            residual(0)
            moe(0)

            ada(1)
            gates("gm1")
            modulate_even("xm1", 1, 0, 8)
            for j in range(KT):
                g = G_AT["qk"] + j
                wait_group(dve, g)
                v.tensor_scalar(qT[:, j, :], ps[g % 8][:, 0:TOK], VT[:, V_BQK + j:V_BQK + j + 1], DH ** -0.5,
                                ALU.add, ALU.mult).then_inc(evacuated[g % 8], 1)
            dve.wait_ge(att_in, 80)
            for n in range(6):
                g = G_AT["v"] + n
                h, t = divmod(n, TT)
                hs = slice(h * 512, (h + 1) * 512)
                wait_group(dve, g)
                v.tensor_tensor(tok[:, t, hs], ps[g % 8][:, :], bv[:, hs], ALU.add).then_inc(evacuated[g % 8], 1)

            units = TT * HEADS

            def maximum(u):
                dve.wait_ge(s_ready, u + 1)
                s = ps[u % 3]
                n = 128
                if u >= HEADS:
                    m = u - HEADS
                    dve.wait_ge(bm_ready, m + 1)
                    link(v.tensor_tensor(s[:, 0:256], s[:, 0:256], bm[:, m % 4, :], ALU.add))
                    n = 384
                v.reduce_max(nmax[:, u:u + 1], s[:, 0:n], AX, negate=True).then_inc(max_ready, 1)

            def heads_out(o):
                dve.wait_ge(p_ready, 8 * o + 8)
                link(v.reciprocal(rden[:, 8 * o:8 * o + 8], den[:, 8 * o:8 * o + 8]))
                dve.wait_ge(pv_done, 8 * o + 8)
                t, h = divmod(o, 2)
                v.tensor_tensor(otok[:, t, h * 512:(h + 1) * 512].rearrange("p (h d) -> p h d", d=DH),
                                ps[5 + o % 3][:, :].rearrange("p (h d) -> p h d", d=DH),
                                rden[:, 8 * o:8 * o + 8].unsqueeze(2).to_broadcast([128, 8, DH]), ALU.mult
                                ).then_inc(o_evac, 1)

            for n in range(units + 5):
                if n < units:
                    maximum(n)
                if n >= 12 and (n - 12) % 8 == 0:
                    heads_out((n - 12) // 8)
            for j in range(KT):
                g = G_AT["ot"] + j
                wait_group(dve, g)
                v.tensor_copy(oT[:, j, :], ps[g % 8][:, 0:TOK]).then_inc(evacuated[g % 8], 1)
            residual(1)
            moe(1)


_INS = ["x_prompt", "x_sample", "cache_k", "cache_v", "c", "c_ctx", "w_ada", "b_ada", "ln_g", "ln_b",
        "hy_w_in", "hy_b_in", "hy_conv_w", "hy_conv_b", "hy_f_w1", "hy_f_b1", "hy_f_w2", "hy_f_b2", "hy_f_w3",
        "hy_f_freq", "hy_decay", "hy_d", "hy_w_out", "hy_b_out",
        "na_w_qkv", "na_b_qkv", "na_rpb", "na_w_out", "na_b_out",
        "moe_w_group", "moe_b_group", "moe_w_expert", "moe_b_expert", "moe_w_up", "moe_w_down"]
_OUTS = [("y_prompt", (1, PROMPT, D)), ("y_sample", (1, SAMPLE, D)),
         ("new_k", (1, 1, HEADS, PROMPT, DH)), ("new_v", (1, 1, HEADS, PROMPT, DH))]


def kernel(**inputs):
    import concourse.bacc as _bacc
    from concourse.bass_utils import run_bass_kernel_spmd as _run

    nc = _bacc.Bacc("TRN2", target_bir_lowering=False, num_devices=1)
    arrays = {n: np.ascontiguousarray(inputs[n]) for n in _INS}
    arrays["na_rpb_rev"] = np.ascontiguousarray(arrays.pop("na_rpb").reshape(HEADS, RPB_H)[:, ::-1])
    arrays.update(shape_constants())
    aps = {n: nc.dram_tensor(f"in_{n}", a.shape, mybir.dt.from_np(a.dtype), kind="ExternalInput").ap()
           for n, a in arrays.items()}
    outs = [nc.dram_tensor(f"out_{n}", s, mybir.dt.float32, kind="ExternalOutput").ap() for n, s in _OUTS]
    build(nc, aps, *outs)
    r = _run(nc, [{f"in_{n}": a for n, a in arrays.items()}], core_ids=[0])
    return tuple(r.results[0][f"out_{n}"] for n, _ in _OUTS)
```
